# Optimizing a Trainium2 kernel written in Bass

```python
import math
import jax
import jax.numpy as jnp
from jax import lax
import numpy as np

D_MODEL = 1024
BATCH = 1
SEQ = 256
DEPTH = 2

GRID_W = 64
CTX_LEN = 256

F_GROUPS = 4
F_DIM = 64
F_WIDTH = F_GROUPS * F_DIM
A_HEADS = 4
A_DH = 64
A_DV = 2 * A_DH
A_QK_WIDTH = A_HEADS * 2 * A_DH
A_WIDTH = A_HEADS * A_DV
Q_BLOCK = 128
ROPE_BASE = 10000.0
G_GROUPS = 4
G_DIM = 64
G_WIDTH = G_GROUPS * G_DIM
CHUNK = 128

MIX_WIDTH = F_WIDTH + A_WIDTH + G_WIDTH
IN_COLS = F_WIDTH + 2 * A_QK_WIDTH + A_WIDTH + 2 * G_WIDTH
COL_SPLITS = [F_WIDTH, F_WIDTH + A_QK_WIDTH, F_WIDTH + 2 * A_QK_WIDTH, F_WIDTH + 2 * A_QK_WIDTH + A_WIDTH]

N_EXPERTS = 16
N_EXPERT_GROUPS = 4
EXPERTS_PER_GROUP = N_EXPERTS // N_EXPERT_GROUPS
TOP_K = 2
D_EXPERT = 512

LN_EPS = 1e-5
RMS_EPS = 1e-5
DEEPNORM_ALPHA = (2 * DEPTH) ** 0.25
DEEPNORM_BETA = (8 * DEPTH) ** -0.25

kernel_name = "hybrid_fourier_diffattn_sgu_moe_dit"

def _layernorm(x, g, b):
    xf = x.astype(jnp.float32)
    mu = jnp.mean(xf, axis=-1, keepdims=True)
    var = jnp.mean(jnp.square(xf - mu), axis=-1, keepdims=True)
    return ((xf - mu) * lax.rsqrt(var + LN_EPS) * g + b).astype(x.dtype)

def _modulate(h, shift, scale):
    return h * (1 + scale) + shift

def _axial_rope_tables(n):
    rows = n // GRID_W
    row = jnp.repeat(jnp.arange(rows, dtype=jnp.float32), GRID_W)
    col = jnp.tile(jnp.arange(GRID_W, dtype=jnp.float32), rows)
    half = A_DH // 2
    inv = ROPE_BASE ** (-jnp.arange(0, half, 2, dtype=jnp.float32) / half)
    ang = jnp.stack([row[:, None] * inv, col[:, None] * inv], axis=1)
    return jnp.cos(ang), jnp.sin(ang)

def _apply_axial_rope(t, cos, sin):
    shp = t.shape
    tr = t.reshape(shp[:-1] + (2, 2, A_DH // 4))
    t1, t2 = tr[..., 0, :], tr[..., 1, :]
    cs, sn = cos[:, None, None], sin[:, None, None]
    out = jnp.stack([t1 * cs - t2 * sn, t1 * sn + t2 * cs], axis=-2)
    return out.reshape(shp).astype(t.dtype)

def _split_groups(p):
    b, n, _ = p.shape
    f, q, k, v, g = jnp.split(p, COL_SPLITS, axis=-1)
    q = q.reshape(b, n, A_HEADS, 2, A_DH)
    k = k.reshape(b, n, A_HEADS, 2, A_DH)
    v = v.reshape(b, n, A_HEADS, A_DV)
    return f, q, k, v, g

def _fourier_mix(f, w):
    b, n, _ = f.shape
    fg = f.reshape(b, n, F_GROUPS, F_DIM).astype(jnp.float32)
    spec = jnp.fft.fftn(fg, axes=(1, 3), norm="ortho").real
    y = jnp.einsum('bngc,gcd->bngd', spec, w.astype(jnp.float32))
    return y.reshape(b, n, F_WIDTH).astype(f.dtype)

def _diff_attn_block(q, k, v, lam):
    s = jnp.einsum('bhcqd,bhckd->bhcqk', q, k).astype(jnp.float32) * (A_DH ** -0.5)
    p = jax.nn.softmax(s, axis=-1)
    a = p[:, :, 0] - lam * p[:, :, 1]
    return jnp.einsum('bhqk,bhkd->bhqd', a.astype(v.dtype), v)

def _latent_diff_attn(q, k_all, v_all, lam):
    b, h, _, n, dh = q.shape
    nb = n // Q_BLOCK
    qb = q.reshape(b, h, 2, nb, Q_BLOCK, dh).transpose(3, 0, 1, 2, 4, 5)
    out = lax.map(lambda qi: _diff_attn_block(qi, k_all, v_all, lam), qb)
    return out.transpose(1, 2, 0, 3, 4).reshape(b, h, n, A_DV)

def _diff_head_norm(o, gain, lam_init):
    of = o.astype(jnp.float32)
    of = of * lax.rsqrt(jnp.mean(of * of, axis=-1, keepdims=True) + RMS_EPS) * gain * (1 - lam_init)
    b, h, n, dv = o.shape
    return of.transpose(0, 2, 1, 3).reshape(b, n, h * dv).astype(o.dtype)

def _to_heads(q, k, v):
    return q.transpose(0, 2, 3, 1, 4), k.transpose(0, 2, 3, 1, 4), v.transpose(0, 2, 1, 3)

def _chunk_sgu(g, ln_g, ln_b, w_s, b_s):
    b, n, _ = g.shape
    g = jax.nn.gelu(g)
    u, v = jnp.split(g, 2, axis=-1)
    v = _layernorm(v, ln_g, ln_b)
    vc = v.reshape(b, n // CHUNK, CHUNK, G_GROUPS, G_DIM)
    mixed = jnp.einsum('bcpgd,gqp->bcqgd', vc, w_s) + jnp.swapaxes(b_s, 0, 1)[:, :, None]
    return u * mixed.reshape(b, n, G_WIDTH)

def _route(h, w_router, router_bias):
    b, t, _ = h.shape
    scores = jax.nn.sigmoid(jnp.einsum('btd,de->bte', h, w_router).astype(jnp.float32))
    sel = scores + router_bias.astype(jnp.float32)
    group_score = jnp.sum(lax.top_k(sel.reshape(b, t, N_EXPERT_GROUPS, EXPERTS_PER_GROUP), TOP_K)[0], axis=-1)
    gidx = jnp.argmax(group_score, axis=-1)
    gmask = gidx[..., None] == jnp.arange(N_EXPERT_GROUPS)
    emask = jnp.repeat(gmask, EXPERTS_PER_GROUP, axis=-1)
    _, idx = lax.top_k(jnp.where(emask, sel, -jnp.inf), TOP_K)
    w = jnp.take_along_axis(scores, idx, axis=-1)
    w = w / jnp.sum(w, axis=-1, keepdims=True)
    return jnp.sum(jax.nn.one_hot(idx, N_EXPERTS, dtype=jnp.float32) * w[..., None], axis=-2)

def _moe(h, gates, w1, w3, w2):
    y = jnp.zeros_like(h)
    for e in range(N_EXPERTS):
        a = jax.nn.silu(h @ w1[e]) * (h @ w3[e])
        y = y + gates[..., e:e + 1].astype(h.dtype) * (a @ w2[e])
    return y

def setup_inputs(seed: int = 0) -> dict:
    key = jax.random.key(seed)
    ks = jax.random.split(key, 22)
    D = D_MODEL
    f32 = jnp.float32

    def nrm(k, shape, scale):
        return jax.random.normal(k, shape, f32) * scale

    return {
        "x": nrm(ks[0], (BATCH, SEQ, D), 1.0),
        "c": nrm(ks[1], (BATCH, D), 1.0),
        "ctx": nrm(ks[2], (BATCH, CTX_LEN, D), 1.0),
        "c_ctx": nrm(ks[3], (D,), 1.0),
        "w_ada": nrm(ks[4], (DEPTH, D, 6 * D), 0.5 * D ** -0.5),
        "b_ada": nrm(ks[5], (DEPTH, 6 * D), 0.02),
        "w_in": nrm(ks[6], (DEPTH, D, IN_COLS), D ** -0.5),
        "w_fourier": nrm(ks[7], (DEPTH, F_GROUPS, F_DIM, F_DIM), F_DIM ** -0.5),
        "diff_lambda": nrm(ks[8], (DEPTH, 4, A_DH), 0.1),
        "diff_subln": 1.0 + nrm(ks[9], (DEPTH, A_DV), 0.02),
        "sgu_ln_g": 1.0 + nrm(ks[10], (DEPTH, G_WIDTH), 0.02),
        "sgu_ln_b": nrm(ks[11], (DEPTH, G_WIDTH), 0.02),
        "sgu_w": nrm(ks[12], (DEPTH, G_GROUPS, CHUNK, CHUNK), CHUNK ** -0.5),
        "sgu_b": 1.0 + nrm(ks[13], (DEPTH, G_GROUPS, CHUNK), 0.02),
        "w_out": nrm(ks[14], (DEPTH, MIX_WIDTH, D), DEEPNORM_BETA * MIX_WIDTH ** -0.5),
        "ln_g": 1.0 + nrm(ks[15], (DEPTH, 2, D), 0.02),
        "ln_b": nrm(ks[16], (DEPTH, 2, D), 0.02),
        "w_router": nrm(ks[17], (D, N_EXPERTS), D ** -0.5),
        "router_bias": nrm(ks[18], (N_EXPERTS,), 0.01),
        "moe_w1": nrm(ks[19], (DEPTH, N_EXPERTS, D, D_EXPERT), D ** -0.5),
        "moe_w3": nrm(ks[20], (DEPTH, N_EXPERTS, D, D_EXPERT), D ** -0.5),
        "moe_w2": nrm(ks[21], (DEPTH, N_EXPERTS, D_EXPERT, D), DEEPNORM_BETA * D_EXPERT ** -0.5),
    }

def reference(x, c, ctx, c_ctx, w_ada, b_ada, w_in, w_fourier, diff_lambda, diff_subln,
              sgu_ln_g, sgu_ln_b, sgu_w, sgu_b, w_out, ln_g, ln_b, w_router, router_bias,
              moe_w1, moe_w3, moe_w2):
    n = x.shape[1]
    cos, sin = _axial_rope_tables(n)
    c_act = jax.nn.silu(c)
    cc_act = jax.nn.silu(c_ctx)
    for l in range(DEPTH):
        last = l == DEPTH - 1
        mod_x = (c_act @ w_ada[l] + b_ada[l])[:, None, :]
        mod_c = cc_act @ w_ada[l] + b_ada[l]
        sh1, sc1, g1, sh2, sc2, g2 = jnp.split(mod_x, 6, axis=-1)
        csh1, csc1, cg1, csh2, csc2, cg2 = jnp.split(mod_c, 6, axis=-1)
        lam_init = 0.8 - 0.6 * math.exp(-0.3 * l)
        lp = diff_lambda[l].astype(jnp.float32)
        lam = jnp.exp(jnp.sum(lp[0] * lp[1])) - jnp.exp(jnp.sum(lp[2] * lp[3])) + lam_init

        px = _modulate(x, sh1, sc1) @ w_in[l]
        pc = _modulate(ctx, csh1, csc1) @ w_in[l]
        fx, qx, kx, vx, gx = _split_groups(px)
        fc, qc, kc, vc, gc = _split_groups(pc)
        qx = _apply_axial_rope(qx, cos, sin)
        kx = _apply_axial_rope(kx, cos, sin)
        qx_h, kx_h, vx_h = _to_heads(qx, kx, vx)
        qc_h, kc_h, vc_h = _to_heads(qc, kc, vc)
        k_all = jnp.concatenate([kc_h, kx_h], axis=3)
        v_all = jnp.concatenate([vc_h, vx_h], axis=2)
        att_x = _diff_head_norm(_latent_diff_attn(qx_h, k_all, v_all, lam), diff_subln[l], lam_init)
        mix_x = jnp.concatenate([
            _fourier_mix(fx, w_fourier[l]),
            att_x,
            _chunk_sgu(gx, sgu_ln_g[l], sgu_ln_b[l], sgu_w[l], sgu_b[l]),
        ], axis=-1)
        x = _layernorm(DEEPNORM_ALPHA * x + g1 * (mix_x @ w_out[l]), ln_g[l, 0], ln_b[l, 0])
        if not last:
            att_c = _diff_head_norm(_diff_attn_block(qc_h, kc_h, vc_h, lam), diff_subln[l], lam_init)
            mix_c = jnp.concatenate([
                _fourier_mix(fc, w_fourier[l]),
                att_c,
                _chunk_sgu(gc, sgu_ln_g[l], sgu_ln_b[l], sgu_w[l], sgu_b[l]),
            ], axis=-1)
            ctx = _layernorm(DEEPNORM_ALPHA * ctx + cg1 * (mix_c @ w_out[l]), ln_g[l, 0], ln_b[l, 0])

        hx = _modulate(x, sh2, sc2)
        yx = _moe(hx, _route(hx, w_router, router_bias), moe_w1[l], moe_w3[l], moe_w2[l])
        x = _layernorm(DEEPNORM_ALPHA * x + g2 * yx, ln_g[l, 1], ln_b[l, 1])
        if not last:
            hc = _modulate(ctx, csh2, csc2)
            yc = _moe(hc, _route(hc, w_router, router_bias), moe_w1[l], moe_w3[l], moe_w2[l])
            ctx = _layernorm(DEEPNORM_ALPHA * ctx + cg2 * yc, ln_g[l, 1], ln_b[l, 1])
    return x


_drawn_inputs = setup_inputs


def setup_inputs(seed=0):
    import zlib

    import numpy as np

    out = dict(_drawn_inputs(seed))
    spreads = {}
    factors = {'b_ada': 2.833,
     'diff_lambda': 8.0,
     'diff_subln': 25.701,
     'sgu_ln_g': 44.147,
     'sgu_ln_b': 36.405,
     'sgu_b': 38.259}
    for name, (base, spread) in spreads.items():
        noise = np.random.default_rng([zlib.crc32(name.encode()), seed]).standard_normal(out[name].shape)
        drawn = base * np.exp(spread * noise) if base else spread * noise
        out[name] = jnp.asarray(drawn.astype(out[name].dtype))
    for name, factor in factors.items():
        out[name] = (out[name] * factor).astype(out[name].dtype)
    return out
```

```python
import math
from contextlib import ExitStack

import numpy as np

import concourse.bass as bass
from concourse import mybir

F32 = mybir.dt.float32
ALU = mybir.AluOpType
ACT = mybir.ActivationFunctionType
AXX = mybir.AxisListType.X

P = 128
D = 1024
KD = D // P
DEPTH = 2
SEQ = 256
GRID_W = 64
HEADS = 4
DH = 64
NEXP = 16
FE = 512
LN_EPS = 1e-5
ALPHA = float((2 * DEPTH) ** 0.25)
SLOTS = 6
SCALE = DH ** -0.5
BIG = 1e30


def tiles(L):
    return 4 if L < DEPTH - 1 else 2


CHUNKS = [("q", 256, 512, tiles), ("k", 768, 512, lambda L: 4), ("g", 1792, 512, tiles),
          ("f", 0, 256, tiles), ("v", 1280, 512, lambda L: 4)]


def units(L):
    return [(t, h) for t in range(tiles(L)) for h in range(HEADS)]


def mod_streams(L, c):
    return (0, 1) if tiles(L) == 4 or c < 4 else (0,)


COUNTS = {
    "h1_ready": lambda L: 4,
    "q_rot": lambda L: 2, "k_rot": lambda L: 2,
    "pad_zero": lambda L: 1,
    "sguv_ready": tiles, "sgu_ready": tiles,
    "bias_ready": lambda L: len(units(L)), "a_ready": lambda L: len(units(L)),
    "on_ready": tiles,
    "var_ready": lambda L: 4 * tiles(L), "rstd_ready": lambda L: 4 * tiles(L),
    "ln1_done": tiles, "hx_ready": tiles, "ln2_done": tiles,
}


def val(name, L, i):
    return sum(COUNTS[name](l) for l in range(L)) + i + 1


def plan_layer(L):
    T = tiles(L)
    jobs = [("ab", L), ("swT", L)]

    def ada(cs):
        out = []
        for n, c in enumerate(cs):
            out.append(("ada", L, c))
            if n:
                out += [("mod", L, cs[n - 1], r) for r in mod_streams(L, cs[n - 1])]
        return out + [("mod", L, cs[-1], r) for r in mod_streams(L, cs[-1])]

    jobs += ada([0, 1, 2, 3])
    jobs += [("hT", L, t, hf) for t in range(4) for hf in range(2)]
    for name, _, _, n in CHUNKS[:4]:
        jobs += [(name, L, t) for t in range(n(L))]
    jobs += [("qT", L, t) for t in range(T)] + [("kT", L, t) for t in range(4)]
    jobs += [("fT", L, t) for t in range(T)]
    jobs += [("v", L, t) for t in range(4)]
    jobs += [("fU", L, t) for t in range(T)]
    jobs += [("fY", L, s, pr) for s in range(T // 2) for pr in range(2)]
    jobs += [("sg", L, t) for t in range(T)]
    U = len(units(L))
    jobs += [("s", L, 0, 0), ("s", L, 0, 1)]
    for u in range(U):
        if u + 1 < U:
            jobs += [("s", L, u + 1, 0), ("s", L, u + 1, 1)]
        jobs += [("aT", L, u), ("pv", L, u)]
    jobs += [("gT", L, t) for t in range(T)] + [("mT", L, t) for t in range(T)]
    jobs += ada([4, 5])
    jobs += [("o", L, hf, t) for hf in range(2) for t in range(T)]
    jobs += ada([6, 7, 8, 9])
    jobs += [("xT", L, t, hf) for t in range(T) for hf in range(2)]
    jobs += [("rt", L, t) for t in range(T)]
    jobs += [("moe", L)]
    jobs += ada([10, 11])
    return jobs


def make_plan():
    fills = [0] * 8
    bank, moe_base = {}, {}
    n = 0
    for L in range(DEPTH):
        for key in plan_layer(L):
            if key[0] == "moe":
                moe_base[L] = list(fills)
                per = NEXP * tiles(L)
                for b in (0, 1, 2, 3, 4, 5):
                    fills[b] += per // 2
                for b in (6, 7):
                    fills[b] += per
                continue
            b = n % 8
            n += 1
            fills[b] += 1
            bank[key] = (b, fills[b])
    return bank, moe_base


def ring_plan():
    order, fill = [], [0] * SLOTS
    place, base = {}, {}
    pos = 0

    def put(key):
        nonlocal pos
        s = pos % SLOTS
        pos += 1
        fill[s] += 1
        place[key] = (s, fill[s])
        order.append(key)

    for L in range(DEPTH):
        for c in range(4):
            put(("ada", L, c))
        for name, *_ in CHUNKS:
            put(("in", L, name))
        put(("ada", L, 4)), put(("ada", L, 5))
        put(("out", L, 0)), put(("out", L, 1))
        for c in range(6, 10):
            put(("ada", L, c))
        pos = -(-pos // SLOTS) * SLOTS
        base[L] = list(fill)
        order.append(("moe", L))
        for s in range(SLOTS):
            fill[s] += NEXP // 2
        put(("ada", L, 10)), put(("ada", L, 11))
    return order, place, base


def constants():
    n = np.arange(SEQ)
    ang = 2 * np.pi * np.outer(n, n) / SEQ
    norm = 1.0 / math.sqrt(SEQ * DH)
    cn, sn = np.cos(ang) * norm, -np.sin(ang) * norm
    m = np.arange(DH)
    a64 = 2 * np.pi * np.outer(m, m) / DH
    blk = lambda w: np.kron(np.eye(2), w)
    half = DH // 2
    inv = (10000.0 ** (-np.arange(0, half, 2, dtype=np.float32) / half)).astype(np.float32)
    row = np.repeat(np.arange(SEQ // GRID_W, dtype=np.float32), GRID_W)
    col = np.tile(np.arange(GRID_W, dtype=np.float32), SEQ // GRID_W)
    an = np.stack([row[:, None] * inv, col[:, None] * inv], 1).astype(np.float64)
    cos, sin = np.cos(an), np.sin(an)
    rc = np.stack([cos, cos], 2).reshape(SEQ, DH)
    rs = np.stack([-sin, sin], 2).reshape(SEQ, DH)
    two = lambda w: w.reshape(2, P, -1).transpose(1, 0, 2).reshape(P, -1)
    sel = np.zeros((P, 2))
    for j in range(4):
        for r in range(2):
            sel[32 * j + r, r] = 1
    parts = {"ident": np.eye(P), "cn": two(cn), "sn": two(sn), "cc": blk(np.cos(a64)), "sc": blk(np.sin(a64)),
             "rc": two(rc), "rs": two(rs), "sel": sel,
             "down16": np.tile(np.arange(16, 0, -1), (P, 1)), "down4": np.tile(np.arange(4, 0, -1), (P, 1))}
    at, cols, o = {}, [], 0
    for k, v in parts.items():
        at[k] = (o, o + v.shape[1])
        o += v.shape[1]
        cols.append(v)
    return np.concatenate(cols, 1).astype(np.float32), at


def backbone(nc, x, c, ctx, c_ctx, w_ada, b_ada, w_in, w_fourier, diff_lambda, diff_subln, sgu_ln_g, sgu_ln_b,
             sgu_w, sgu_b, w_out, ln_g, ln_b, w_router, router_bias, moe_w1, moe_w3, moe_w2, const, out):
    CAT = constants()[1]
    BANK, MOE_BASE = make_plan()
    RING, PLACE, RING_BASE = ring_plan()
    NCONST = const.shape[1]
    LAM_INIT = [0.8 - 0.6 * math.exp(-0.3 * l) for l in range(DEPTH)]

    es = ExitStack()
    with es:
        def sb(name, shape):
            return es.enter_context(nc.sbuf_tensor(name, shape, F32))

        def sem(name):
            return es.enter_context(nc.semaphore(name))

        X = sb("X", [P, 4, D])
        H = sb("H", [P, 4 * D])
        XT = sb("XT", [P, KD, 512])
        RA = sb("RA", [P, 2048])
        RB = sb("RB", [P, 2048])
        RC = sb("RC", [P, 2048])
        KT = sb("KT", [P, 2048])
        EX = sb("EX", [P, 4, 512])
        AT = sb("AT", [P, 2, 512])
        W = sb("W", [P, SLOTS, 4096])
        R4 = sb("R4", [P, 2, 512])
        CT = sb("CT", [P, KD, 32])
        CR = sb("CR", [P, 2, KD])
        CE = sb("CE", [P, 2, KD])
        C = sb("C", [P, NCONST])
        BA = sb("BA", [12, 512])
        WF = sb("WF", [P, 2, P])
        AB = sb("AB", [P, 2, 2, P])
        SWT = sb("SWT", [P, 4, P])
        LM = sb("LM", [P, 4, DH])
        GAIN = sb("GAIN", [P, P])
        SG = sb("SG", [P, 2, 256])
        SB_ = sb("SB_", [P, 4])
        WR = sb("WR", [P, KD, NEXP])
        RBIAS = sb("RBIAS", [P, NEXP])
        JUNK = sb("JUNK", [P, P])
        ST = sb("ST", [P, 2, 6])
        MV = sb("MV", [P, 4, 2])
        VAR = sb("VAR", [P, 24, 4])
        RSTD = sb("RSTD", [P, 24, 4])
        HALF = sb("HALF", [P, 4])
        LAM = sb("LAM", [P, 8])
        MX = sb("MX", [P, 2, 2])
        NB = sb("NB", [P, 2, 2])
        SM = sb("SM", [P, 2, 2])
        RI = sb("RI", [P, 2, 2])
        SS = sb("SS", [P, 4, HEADS])
        ER = sb("ER", [P, 4, NEXP])
        SCO = sb("SCO", [P, 4, NEXP])
        SEL = sb("SEL", [P, 4, NEXP])
        WK = sb("WK", [P, 4, NEXP])
        OH = sb("OH", [P, 4, NEXP])
        GATE = sb("GATE", [P, 4, NEXP])
        PG = sb("PG", [P, 4, 6, 4])
        GS = sb("GS", [P, 4, 4])
        GM = sb("GM", [P, 4, 4])
        T1 = sb("T1", [P, 4, 1])
        PS = es.enter_context(nc.psum_tensor("PS", [P, 8, 512], F32))

        def cst(name):
            a, b = CAT[name]
            return C[:, a:b]

        IDENT = cst("ident")
        SH = RA[:, :].rearrange("p (s d) -> p s d", s=2)
        SCL = RB[:, :].rearrange("p (s d) -> p s d", s=2)
        GT = RC[:, :].rearrange("p (s d) -> p s d", s=2)
        VEC = [SH, SCL, GT, SH, SCL, GT]
        HR = H[:, :].rearrange("p (t d) -> p t d", t=4)
        QT = H[:, :].rearrange("p (c h t) -> p c h t", c=2, h=HEADS)
        QR = RA[:, :].rearrange("p (t d) -> p t d", t=4)
        VR = QR
        KR = RB[:, :].rearrange("p (t d) -> p t d", t=4)
        FT = RB[:, 0:1024].rearrange("p (t a c) -> p t a c", t=4, a=2)
        OB = KR
        GR = RC[:, :].rearrange("p (t d) -> p t d", t=4)
        KTv = KT[:, :].rearrange("p (h t) -> p h t", h=HEADS)
        LNR = KT[:, :].rearrange("p (a d) -> p a d", a=2)
        FR = AT[:, :, :].rearrange("p a (b d) -> p (a b) d", b=2)
        U = EX[:, :, :].rearrange("p t (a b c) -> p t a b c", a=2, b=2)
        SWR = RC[:, 0:512].rearrange("p (g q) -> p g q", g=4)

        bank_full = [sem(f"bank_full{b}") for b in range(8)]
        bank_free = [sem(f"bank_free{b}") for b in range(8)]
        w_full = [sem(f"w_full{s}") for s in range(SLOTS)]
        S = {name: sem(name) for name in COUNTS}
        x_in = sem("x_in")
        const_in = sem("const_in")
        c_in = sem("c_in")
        router_in = sem("router_in")
        layer_in = sem("layer_in")
        layer_small_in = sem("layer_small_in")
        wf_zero = sem("wf_zero")
        ln_in = sem("ln_in")
        lamgain_ready = sem("lamgain_ready")
        setup_ready = sem("setup_ready")
        cexp_ready = sem("cexp_ready")
        cT_ready = sem("cT_ready")
        dve_step = sem("dve_step")
        act_step = sem("act_step")
        pool_step = sem("pool_step")
        out_written = sem("out_written")
        lam_exp = sem("lam_exp")
        lam_sum = sem("lam_sum")
        LAYER_DMAS = 6
        WF_DMAS = 5

        def full(eng, key):
            b, n = BANK[key]
            eng.wait_ge(bank_full[b], n)
            return PS[:, b, :]

        def freed(key):
            return bank_free[BANK[key][0]]

        def read(eng, key):
            b, n = BANK[key]
            eng.wait_ge(bank_free[b], n)

        w_src = {}
        for L in range(DEPTH):
            for n in range(12):
                w_src["ada", L, n] = (w_ada[L, :, 512 * n:512 * n + 512], 512)
            for name, c0, cw, _ in CHUNKS:
                w_src["in", L, name] = (w_in[L, :, c0:c0 + cw], cw)
            for hf in range(2):
                w_src["out", L, hf] = (w_out[L, :, 512 * hf:512 * hf + 512], 512)

        def slot(key):
            s = PLACE[key][0]
            cw = w_src[key][1]
            return W[:, s, 0:KD * cw].rearrange("p (k n) -> p k n", k=KD)

        def moe_up(s):
            return W[:, s, :].rearrange("p (k n) -> p k n", k=KD)

        def moe_down(s):
            return W[:, s, :].rearrange("p (k n) -> p k n", k=FE // P)

        def last_job(key):
            kind, L, n = key
            if kind == "ada":
                return key
            if kind == "in":
                return (n, L, {ch[0]: ch[3] for ch in CHUNKS}[n](L) - 1)
            return ("o", L, n, tiles(L) - 1)

        def req(L, kind, t):
            order = ["sgu", "att", "ln1", "ln2"]
            return sum(4 * tiles(l) for l in range(L)) + order.index(kind) * tiles(L) + t

        block = es.enter_context(nc.Block())

        @block.sync
        def _(sp):
            def moe_load(L, e, n, at):
                s = 3 * e + n
                k = KD if n < 2 else FE // P
                dst = W[:, s, :].rearrange("p (k n) -> p k n", k=k)
                src = (moe_w1, moe_w3, moe_w2)[n][L, at, :, :]
                src = src.rearrange("(k p) n -> p k n", p=P) if isinstance(at, int) else \
                    src.rearrange("o (k p) n -> p (o k) n", p=P)
                sp.dma_start(dst, src).then_inc(w_full[s], 16)

            last = [None] * SLOTS
            for key in RING:
                if key[0] == "moe":
                    L = key[1]
                    T = tiles(L)
                    mb = MOE_BASE[L]
                    for s in range(SLOTS):
                        full(sp, last[s])
                        moe_load(L, s // 3, s % 3, s // 3)
                    with sp.Fori(1, NEXP // 2) as i:
                        for e in range(2):
                            for n in range(3):
                                if n < 2:
                                    sp.wait_ge(bank_full[2 + n], i * T + (mb[2 + n] - T + ((e + 1) * T) // 2))
                                else:
                                    sp.wait_ge(bank_full[7], i * 2 * T + (mb[7] - 2 * T + (e + 1) * T))
                                moe_load(L, e, n, bass.ds(2 * i + e, 1))
                    last = [("moe", L)] * SLOTS
                    continue
                s, n = PLACE[key]
                if last[s] and last[s][0] == "moe":
                    L0 = last[s][1]
                    n_, e_ = s % 3, s // 3
                    T0, mb = tiles(L0), MOE_BASE[L0]
                    last_it = NEXP // 2 - 1
                    if n_ < 2:
                        sp.wait_ge(bank_full[2 + n_], mb[2 + n_] + last_it * T0 + ((e_ + 1) * T0) // 2)
                    else:
                        sp.wait_ge(bank_full[7], mb[7] + last_it * 2 * T0 + (e_ + 1) * T0)
                elif last[s]:
                    full(sp, last[s])
                sp.dma_start(slot(key), w_src[key][0].rearrange("(k p) n -> p k n", p=P)).then_inc(w_full[s], 16)
                last[s] = last_job(key)

        @block.gpsimd
        def _(pool):
            pool.memset(HALF[:, :], -0.5).then_inc(pool_step, 1)
            pool.wait_ge(pool_step, 1)

            def params(L):
                if L:
                    pool.wait_ge(S["on_ready"], val("on_ready", L - 1, tiles(L - 1) - 1))
                    pool.wait_ge(S["sgu_ready"], val("sgu_ready", L - 1, tiles(L - 1) - 1))
                    full(pool, ("ada", L - 1, 11))
                    pool.wait_ge(S["ln2_done"], val("ln2_done", L - 1, tiles(L - 1) - 1))
                pool.dma_start(BA[:, :], b_ada[L].rearrange("(c n) -> c n", n=512)).then_inc(layer_small_in, 16)
                pool.dma_start(LM[:, :, :].rearrange("p a d -> p (a d)"),
                               diff_lambda[L].rearrange("a d -> (a d)").partition_broadcast(P)).then_inc(layer_small_in, 16)
                pool.dma_start(GAIN[:, :], diff_subln[L].partition_broadcast(P)).then_inc(layer_small_in, 16)
                pool.dma_start(SG[:, 0, :], sgu_ln_g[L].partition_broadcast(P)).then_inc(layer_small_in, 16)
                pool.dma_start(SG[:, 1, :], sgu_ln_b[L].partition_broadcast(P)).then_inc(layer_small_in, 16)
                with nc.allow_non_contiguous_dma("512 words"):
                    pool.dma_start(SB_[:, :], sgu_b[L].rearrange("g q -> q g")).then_inc(layer_small_in, 16)
                if L == 0:
                    pool.wait_ge(wf_zero, 1)
                for g in range(4):
                    o = 64 * (g % 2)
                    pool.dma_start(WF[o:o + 64, g // 2, o:o + 64], w_fourier[L, g]).then_inc(layer_in, 16)
                pool.dma_start(SWR, sgu_w[L].rearrange("g q p -> q g p")).then_inc(layer_in, 16)

            def rstds(L, kind):
                for t in range(tiles(L)):
                    r = req(L, kind, t)
                    n = HEADS if kind == "att" else 1
                    pool.wait_ge(S["var_ready"], r + 1)
                    pool.tensor_tensor(RSTD[:, r, 0:n], VAR[:, r, 0:n], HALF[:, 0:n], ALU.pow).then_inc(S["rstd_ready"], 1)

            for L in range(DEPTH):
                params(L)
                full(pool, ("hT", L, 3, 1))
                pool.memset(QT[64:128, 0, :, :].rearrange("p h t -> p (h t)"), 0.0).then_inc(pool_step, 1)
                pool.wait_ge(pool_step, L + 2)
                pool.memset(QT[0:64, 1, :, :].rearrange("p h t -> p (h t)"), 0.0).then_inc(S["pad_zero"], 1)
                pool.wait_ge(S["pad_zero"], val("pad_zero", L, 0))
                rstds(L, "sgu")
                rstds(L, "att")
                for j in range(2):
                    if j == 0:
                        full(pool, ("s", L, len(units(L)) - 1, 1))
                    else:
                        pool.wait_ge(S["ln1_done"], val("ln1_done", L, tiles(L) - 1))
                    pool.dma_start(LNR[:, 0, :], ln_g[L, j].partition_broadcast(P)).then_inc(ln_in, 16)
                    pool.dma_start(LNR[:, 1, :], ln_b[L, j].partition_broadcast(P)).then_inc(ln_in, 16)
                    rstds(L, ("ln1", "ln2")[j])

        @block.scalar
        def _(act):
            with nc.allow_non_contiguous_dma("two vectors, as columns"):
                act.dma_start(CR[:, 0, :], c[0].rearrange("(k p) -> p k", p=P)).then_inc(c_in, 16)
                act.dma_start(CR[:, 1, :], c_ctx.rearrange("(k p) -> p k", p=P)).then_inc(c_in, 16)
            act.dma_start(C[:, :], const).then_inc(const_in, 16)
            act.dma_start(X[:, 0:2, :], x[0].rearrange("(t p) d -> p t d", p=P)).then_inc(x_in, 16)
            act.dma_start(X[:, 2:4, :], ctx[0].rearrange("(t p) d -> p t d", p=P)).then_inc(x_in, 16)
            act.dma_start(WR[:, :, :], w_router.rearrange("(k p) e -> p k e", p=P)).then_inc(router_in, 16)
            act.dma_start(RBIAS[:, :], router_bias.partition_broadcast(P)).then_inc(router_in, 16)
            act.wait_ge(c_in, 32)
            nc.scalar.activation(CE[:, :, :], CR[:, :, :], ACT.Exp, scale=-1.0).then_inc(cexp_ready, 1)

            def copy(dst, src, done):
                nc.scalar.activation(dst, src, ACT.Copy).then_inc(done, 1)

            def mods(L, cs):
                for c_ in cs:
                    for r in mod_streams(L, c_):
                        v, hf = c_ // 2, c_ % 2
                        key = ("mod", L, c_, r)
                        ps = full(act, key)
                        if v == 0 and L and hf == 0 and r == 0:
                            act.wait_ge(S["hx_ready"], val("hx_ready", L - 1, tiles(L - 1) - 1))
                        if v == 5 and hf == 0 and r == 0:
                            act.wait_ge(S["ln1_done"], val("ln1_done", L, tiles(L) - 1))
                        copy(VEC[v][:, r, 512 * hf:512 * hf + 512], ps, freed(key))

            for L in range(DEPTH):
                T = tiles(L)
                act.wait_ge(lam_sum, L + 1)
                nc.scalar.activation(LAM[:, 2:4], LAM[:, 0:2], ACT.Exp).then_inc(lam_exp, 1)
                mods(L, [0, 1, 2, 3])
                for t in range(4):
                    for hf in range(2):
                        key = ("hT", L, t, hf)
                        ps = full(act, key)
                        if L and t == 0 and hf == 0:
                            full(act, ("ada", L - 1, 10))
                        copy(XT[:, 4 * hf:4 * hf + 4, P * t:P * t + P], ps.rearrange("p (k t) -> p k t", k=4), freed(key))
                for t in range(T):
                    key = ("q", L, t)
                    ps = full(act, key)
                    if t == 0:
                        act.wait_ge(S["h1_ready"], val("h1_ready", L, 3))
                    copy(QR[:, t, :], ps, freed(key))
                for t in range(4):
                    key = ("k", L, t)
                    copy(KR[:, t, :], full(act, key), freed(key))
                for t in range(T):
                    key = ("g", L, t)
                    ps = full(act, key)
                    nc.scalar.activation(GR[:, t, :], ps, ACT.Gelu_apprx_tanh)\
                        .then_inc(freed(key), 1)
                for t in range(T):
                    key = ("f", L, t)
                    copy(FR[:, t, :], full(act, key)[:, 0:256], freed(key))
                act.wait_ge(S["pad_zero"], val("pad_zero", L, 0))
                for t in range(T):
                    key = ("qT", L, t)
                    ps = full(act, key).rearrange("p (h t) -> p h t", h=HEADS)
                    for cc in range(2):
                        a = 64 * cc
                        ins = nc.scalar.activation(QT[a:a + 64, cc, :, P * t:P * t + P], ps[a:a + 64], ACT.Copy)
                    ins.then_inc(freed(key), 1)
                for t in range(T):
                    key = ("fT", L, t)
                    copy(FT[:, t, :, :], full(act, key)[:, 0:256].rearrange("p (a c) -> p a c", a=2), freed(key))
                for t in range(4):
                    key = ("v", L, t)
                    copy(VR[:, t, :], full(act, key), freed(key))
                for s in range(T // 2):
                    for pr in range(2):
                        key = ("fY", L, s, pr)
                        copy(XT[:, pr, SEQ * s:SEQ * s + SEQ], full(act, key)[:, 0:SEQ], freed(key))
                UN = units(L)

                def exps(u):
                    t, h = UN[u]
                    nk = 512 if t < 2 else 256
                    act.wait_ge(S["bias_ready"], val("bias_ready", L, u))
                    if u >= 2:
                        full(act, ("aT", L, u - 2))
                    for cc in range(2):
                        key = ("s", L, u, cc)
                        ps = full(act, key)
                        ins = nc.scalar.activation(EX[:, 2 * (u % 2) + cc, 0:nk], ps[:, 0:nk], ACT.Exp,
                                                   bias=NB[:, u % 2, cc:cc + 1], scale=SCALE,
                                                   accum_out=SM[:, u % 2, cc:cc + 1]).then_inc(freed(key), 1)

                def evacuate(u):
                    t, h = UN[u]
                    nk = 512 if t < 2 else 256
                    key = ("aT", L, u)
                    ps = full(act, key)
                    if u >= 2:
                        full(act, ("pv", L, u - 2))
                    copy(AT[:, u % 2, 0:nk], ps[:, 0:nk], freed(key))
                    key = ("pv", L, u)
                    ps = full(act, key)
                    nc.scalar.activation(OB[:, t, P * h:P * h + P], ps[:, 0:P], ACT.Copy)
                    if u:
                        read(act, ("pv", L, u - 1))
                    nc.scalar.activation(JUNK[:, :], ps[:, 0:P], ACT.Square, accum_out=SS[:, t, h:h + 1])\
                        .then_inc(freed(key), 1)

                exps(0)
                for u in range(len(UN)):
                    if u + 1 < len(UN):
                        exps(u + 1)
                    evacuate(u)
                for t in range(T):
                    key = ("gT", L, t)
                    copy(XT[:, 6:8, P * t:P * t + P], full(act, key)[:, 0:256].rearrange("p (k t) -> p k t", k=2), freed(key))
                for t in range(T):
                    key = ("mT", L, t)
                    copy(XT[:, 2:6, P * t:P * t + P], full(act, key).rearrange("p (k t) -> p k t", k=4), freed(key))
                mods(L, [4, 5])
                mods(L, [6, 7, 8, 9])
                for t in range(T):
                    for hf in range(2):
                        key = ("xT", L, t, hf)
                        copy(XT[:, 4 * hf:4 * hf + 4, P * t:P * t + P],
                             full(act, key).rearrange("p (k t) -> p k t", k=4), freed(key))
                for t in range(T):
                    key = ("rt", L, t)
                    ps = full(act, key)
                    nc.scalar.activation(ER[:, t, :], ps[:, 0:NEXP], ACT.Exp, scale=-1.0)\
                        .then_inc(freed(key), 1)
                N = 2 * T
                mb = MOE_BASE[L]
                with act.Fori(0, NEXP // 2) as i:
                    def silu(j):
                        b = 2 * (j % 2)
                        act.wait_ge(bank_full[b], i * T + (mb[b] + j // 2 + 1))
                        act.wait_ge(bank_free[b + 1], i * T + (mb[b + 1] + j // 2))
                        nc.scalar.activation(EX[:, j % 2, :], PS[:, b, :], ACT.Silu).then_inc(bank_free[b], 1)

                    def turn(j):
                        b = 4 + j % 2
                        act.wait_ge(bank_full[b], i * T + (mb[b] + j // 2 + 1))
                        act.wait_ge(bank_full[7], i * N + (mb[7] + j - 1))
                        nc.scalar.activation(AT[:, j % 2, :], PS[:, b, :], ACT.Copy).then_inc(bank_free[b], 1)

                    silu(0)
                    for j in range(N):
                        if j + 1 < N:
                            silu(j + 1)
                        turn(j)
                mods(L, [10, 11])
            for t in range(2):
                act.wait_ge(S["ln2_done"], val("ln2_done", DEPTH - 1, t))
                act.dma_start(out[0, P * t:P * t + P, :], X[:, t, :]).then_inc(out_written, 16)
            act.wait_ge(out_written, 32)

        @block.vector
        def _(dve):
            steps = [0]

            def link(ins):
                steps[0] += 1
                ins.then_inc(dve_step, 1)
                dve.wait_ge(dve_step, steps[0])

            dve.memset(WF[:, :, :].rearrange("p a b -> p (a b)"), 0.0).then_inc(wf_zero, 1)
            link(dve.memset(CT[:, :, :].rearrange("p a b -> p (a b)"), 0.0))
            dve.wait_ge(c_in, 32)
            dve.wait_ge(cexp_ready, 1)
            link(dve.tensor_scalar(CE[:, :, :], CE[:, :, :], 1.0, None, ALU.add))
            link(dve.reciprocal(CE[:, :, :], CE[:, :, :]))
            dve.tensor_tensor(CT[:, :, 0:2].rearrange("p k s -> p s k"), CE[:, :, :], CR[:, :, :], ALU.mult).then_inc(cT_ready, 1)

            def lam(L):
                dve.wait_ge(layer_small_in, 16 * LAYER_DMAS * (L + 1))
                for j in range(2):
                    link(dve.tensor_tensor(JUNK2, LM[:, 2 * j, :], LM[:, 2 * j + 1, :], ALU.mult))
                    ins = dve.tensor_reduce(LAM[:, j:j + 1], JUNK2, AXX, ALU.add)
                    if j == 0:
                        link(ins)
                ins.then_inc(lam_sum, 1)
                dve.wait_ge(lam_exp, L + 1)
                link(dve.tensor_tensor(LAM[:, 4:5], LAM[:, 2:3], LAM[:, 3:4], ALU.subtract))
                link(dve.tensor_scalar(LAM[:, 5:6], LAM[:, 4:5], LAM_INIT[L], None, ALU.add))
                link(dve.tensor_scalar(GAIN[:, :], GAIN[:, :], 1.0 - LAM_INIT[L], None, ALU.mult))

            JUNK2 = JUNK[:, 0:DH]

            def ada_copy(L, cs):
                for c_ in cs:
                    key = ("ada", L, c_)
                    ps = full(dve, key)
                    if c_ >= 2 or L:
                        pc, pL = (c_ - 2, L) if c_ >= 2 else (c_ + 10, L - 1)
                        full(dve, ("mod", pL, pc, mod_streams(pL, pc)[-1]))
                    dve.tensor_copy(R4[:, c_ % 2, :], ps).then_inc(freed(key), 1)

            def modulate(L, t, buf_sh, buf_sc, done):
                s = t // 2
                link(dve.scalar_tensor_tensor(out=HR[:, t, :], in0=buf_sc[:, s, :], scalar=1.0, in1=X[:, t, :],
                                              op0=ALU.add, op1=ALU.mult))
                dve.tensor_tensor(HR[:, t, :], HR[:, t, :], buf_sh[:, s, :], ALU.add).then_inc(done, 1)

            def ask(r, n, src, scale, eps):
                dve.tensor_scalar(VAR[:, r, 0:n], src, scale, eps, ALU.mult, ALU.add).then_inc(S["var_ready"], 1)

            def stats(L, kind, t):
                for hf in range(2):
                    ins = dve.bn_stats(ST[:, hf, :], X[:, t, 512 * hf:512 * hf + 512])
                link(ins)
                link(dve.bn_aggr(MV[:, t, :], ST[:, :, :].rearrange("p a b -> p (a b)")))
                ask(req(L, kind, t), 1, MV[:, t, 1:2], 1.0, LN_EPS)

            def normalise(L, kind, t, done):
                r = req(L, kind, t)
                dve.wait_ge(S["rstd_ready"], r + 1)
                link(dve.tensor_scalar(X[:, t, :], X[:, t, :], MV[:, t, 0:1], RSTD[:, r, 0:1], ALU.subtract, ALU.mult))
                j = 0 if kind == "ln1" else 1
                dve.wait_ge(ln_in, 32 * (2 * L + j + 1))
                link(dve.tensor_tensor(X[:, t, :], X[:, t, :], LNR[:, 0, :], ALU.mult))
                ins = dve.tensor_tensor(X[:, t, :], X[:, t, :], LNR[:, 1, :], ALU.add)
                ins.then_inc(done, 1)

            def rotate(R, t):
                a, b = CAT["rc"][0] + DH * t, CAT["rs"][0] + DH * t
                cos = C[:, a:a + DH].unsqueeze(1).to_broadcast([P, 8, DH])
                rows = R[:, t, :].rearrange("p (n d) -> p n d", d=DH)
                dve.tensor_tensor(EX[:, 0, :].rearrange("p (n d) -> p n d", d=DH), rows, cos, ALU.mult)
                for o in range(2):
                    sw = R[:, t, :].rearrange("p (n a b i) -> p n a b i", a=2, b=2, i=16)[:, :, :, 1 - o, :]
                    sn = C[:, b:b + DH].rearrange("p (a b i) -> p a b i", a=2, b=2)[:, :, o, :]
                    sn = sn.unsqueeze(1).to_broadcast([P, 8, 2, 16])
                    dst = EX[:, 1, :].rearrange("p (n a b i) -> p n a b i", a=2, b=2, i=16)[:, :, :, o, :]
                    ins = dve.tensor_tensor(dst, sw, sn, ALU.mult)
                link(ins)
                return dve.tensor_tensor(R[:, t, :], EX[:, 0, :], EX[:, 1, :], ALU.add)

            for L in range(DEPTH):
                T = tiles(L)
                key = ("ab", L)
                dve.tensor_copy(AB[:, :, :, :].rearrange("p a b c -> p (a b c)"), full(dve, key))\
                    .then_inc(freed(key), 1)
                key = ("swT", L)
                dve.tensor_copy(SWT[:, :, :].rearrange("p a b -> p (a b)"), full(dve, key))\
                    .then_inc(freed(key), 1)
                lam(L)
                ada_copy(L, [0, 1, 2, 3])
                if L == 0:
                    dve.wait_ge(x_in, 32)
                for c_ in range(4):
                    for r in (0, 1):
                        read(dve, ("mod", L, c_, r))
                for t in range(4):
                    modulate(L, t, SH, SCL, S["h1_ready"])
                dve.wait_ge(const_in, 16)
                for t in range(2):
                    read(dve, ("q", L, t))
                    if t:
                        dve.wait_ge(S["q_rot"], val("q_rot", L, t - 1))
                    rotate(QR, t).then_inc(S["q_rot"], 1)
                for t in range(2):
                    read(dve, ("k", L, t))
                    if t:
                        dve.wait_ge(S["k_rot"], val("k_rot", L, t - 1))
                    else:
                        dve.wait_ge(S["q_rot"], val("q_rot", L, 1))
                    rotate(KR, t).then_inc(S["k_rot"], 1)
                for t in range(4):
                    key = ("kT", L, t)
                    ps = full(dve, key)
                    if L and t == 0:
                        dve.wait_ge(S["ln2_done"], val("ln2_done", L - 1, tiles(L - 1) - 1))
                    dve.tensor_copy(KTv[:, :, P * t:P * t + P], ps.rearrange("p (h t) -> p h t", h=HEADS))\
                        .then_inc(freed(key), 1)
                for t in range(T):
                    read(dve, ("g", L, t))
                    link(dve.bn_stats(ST[:, 0, :], GR[:, t, 256:512]))
                    link(dve.bn_aggr(MV[:, t, :], ST[:, 0, :]))
                    ask(req(L, "sgu", t), 1, MV[:, t, 1:2], 1.0, LN_EPS)
                for t in range(T):
                    r = req(L, "sgu", t)
                    dve.wait_ge(S["rstd_ready"], r + 1)
                    v = GR[:, t, 256:512]
                    link(dve.tensor_scalar(v, v, MV[:, t, 0:1], RSTD[:, r, 0:1], ALU.subtract, ALU.mult))
                    link(dve.tensor_tensor(v, v, SG[:, 0, :], ALU.mult))
                    dve.tensor_tensor(v, v, SG[:, 1, :], ALU.add).then_inc(S["sguv_ready"], 1)
                for t in range(T):
                    key = ("fU", L, t)
                    dve.tensor_copy(U[:, t, :, :, :].rearrange("p a b c -> p (a b c)"), full(dve, key))\
                        .then_inc(freed(key), 1)
                for t in range(T):
                    key = ("sg", L, t)
                    ps = full(dve, key)[:, 0:256].rearrange("p (g d) -> p g d", g=4)
                    m = GR[:, t, 256:512]
                    ins = dve.tensor_tensor(m.rearrange("p (g d) -> p g d", g=4), ps,
                                            SB_[:, :].unsqueeze(2).to_broadcast([P, 4, 64]), ALU.add)
                    ins.then_inc(freed(key), 1)
                    read(dve, key)
                    dve.tensor_tensor(GR[:, t, 0:256], GR[:, t, 0:256], m, ALU.mult).then_inc(S["sgu_ready"], 1)
                UN = units(L)

                def maxima(u):
                    nk = 512 if UN[u][0] < 2 else 256
                    if u >= 2:
                        read(dve, ("s", L, u - 2, 1))
                        dve.wait_ge(S["bias_ready"], val("bias_ready", L, u - 2))
                    for cc in range(2):
                        ps = full(dve, ("s", L, u, cc))
                        ins = dve.tensor_reduce(MX[:, u % 2, cc:cc + 1], ps[:, 0:nk], AXX, ALU.max)
                    link(ins)
                    dve.tensor_scalar(NB[:, u % 2, :], MX[:, u % 2, :], -SCALE, None, ALU.mult)\
                        .then_inc(S["bias_ready"], 1)

                def combine(u):
                    nk = 512 if UN[u][0] < 2 else 256
                    p = u % 2
                    for cc in range(2):
                        read(dve, ("s", L, u, cc))
                    if u >= 2:
                        dve.wait_ge(S["a_ready"], val("a_ready", L, u - 2))
                    link(dve.reciprocal(RI[:, p, :], SM[:, p, :]))
                    e0, e1 = EX[:, 2 * p, 0:nk], EX[:, 2 * p + 1, 0:nk]
                    link(dve.tensor_scalar(e1, e1, RI[:, p, 1:2], LAM[:, 5:6], ALU.mult, ALU.mult))
                    dve.scalar_tensor_tensor(out=e0, in0=e0, scalar=RI[:, p, 0:1], in1=e1,
                                             op0=ALU.mult, op1=ALU.subtract).then_inc(S["a_ready"], 1)

                maxima(0)
                for u in range(len(UN)):
                    if u + 1 < len(UN):
                        maxima(u + 1)
                    combine(u)
                for t in range(T):
                    for h in range(HEADS):
                        read(dve, ("pv", L, HEADS * t + h))
                    ask(req(L, "att", t), HEADS, SS[:, t, :], 1.0 / P, LN_EPS)
                for t in range(T):
                    r = req(L, "att", t)
                    dve.wait_ge(S["rstd_ready"], r + 1)
                    for h in range(HEADS):
                        o = OB[:, t, P * h:P * h + P]
                        ins = dve.scalar_tensor_tensor(out=o, in0=o, scalar=RSTD[:, r, h:h + 1], in1=GAIN[:, :],
                                                       op0=ALU.mult, op1=ALU.mult)
                    ins.then_inc(S["on_ready"], 1)
                ada_copy(L, [4, 5])
                for hf in range(2):
                    for r in mod_streams(L, 4 + hf):
                        read(dve, ("mod", L, 4 + hf, r))
                    cs = slice(512 * hf, 512 * hf + 512)
                    for t in range(T):
                        key = ("o", L, hf, t)
                        ps = full(dve, key)
                        dve.tensor_tensor(HR[:, t, cs], ps, GT[:, t // 2, cs], ALU.mult).then_inc(freed(key), 1)
                        read(dve, key)
                        ins = dve.scalar_tensor_tensor(out=X[:, t, cs], in0=X[:, t, cs], scalar=ALPHA,
                                                       in1=HR[:, t, cs], op0=ALU.mult, op1=ALU.add)
                link(ins)
                ada_copy(L, [6, 7, 8, 9])
                for t in range(T):
                    stats(L, "ln1", t)
                for t in range(T):
                    normalise(L, "ln1", t, S["ln1_done"])
                dve.wait_ge(S["ln1_done"], val("ln1_done", L, T - 1))
                for c_ in range(6, 10):
                    for r in mod_streams(L, c_):
                        read(dve, ("mod", L, c_, r))
                for t in range(T):
                    modulate(L, t, SH, SCL, S["hx_ready"])
                for t in range(T):
                    read(dve, ("rt", L, t))
                if L == 0:
                    dve.wait_ge(router_in, 32)
                sc, sl, wk, oh, ga = (b[:, 0:T, :] for b in (SCO, SEL, WK, OH, GATE))
                t1 = T1[:, 0:T, :]
                bc16 = lambda a: a.to_broadcast([P, T, NEXP])
                down16 = cst("down16").unsqueeze(1).to_broadcast([P, T, NEXP])
                down4 = cst("down4").unsqueeze(1).to_broadcast([P, T, 4])
                link(dve.tensor_scalar(sc, ER[:, 0:T, :], 1.0, None, ALU.add))
                link(dve.reciprocal(sc, sc))
                link(dve.tensor_tensor(sl, sc, RBIAS[:, :].unsqueeze(1).to_broadcast([P, T, NEXP]), ALU.add))
                s4 = sl.rearrange("p t (g e) -> p t g e", g=4)
                for n, (a, b) in enumerate([(0, 1), (0, 2), (0, 3), (1, 2), (1, 3), (2, 3)]):
                    ins = dve.tensor_tensor(PG[:, 0:T, n, :], s4[:, :, :, a], s4[:, :, :, b], ALU.add)
                link(ins)
                for n in range(1, 6):
                    link(dve.tensor_tensor(PG[:, 0:T, 0, :], PG[:, 0:T, 0, :], PG[:, 0:T, n, :], ALU.max))
                gs, gm = GS[:, 0:T, :], GM[:, 0:T, :]

                def first_best(src, n, down, w, one_hot):
                    link(dve.tensor_reduce(t1, src, AXX, ALU.max))
                    link(dve.tensor_tensor(w, src, t1.to_broadcast([P, T, n]), ALU.is_equal))
                    link(dve.tensor_tensor(w, w, down, ALU.mult))
                    link(dve.tensor_reduce(t1, w, AXX, ALU.max))
                    link(dve.tensor_tensor(one_hot, w, t1.to_broadcast([P, T, n]), ALU.is_equal))

                first_best(PG[:, 0:T, 0, :], 4, down4, gs, gm)
                link(dve.tensor_tensor(s4, s4, gm.unsqueeze(3).to_broadcast([P, T, 4, 4]), ALU.mult))
                link(dve.tensor_scalar(gm, gm, BIG, -BIG, ALU.mult, ALU.add))
                link(dve.tensor_tensor(s4, s4, gm.unsqueeze(3).to_broadcast([P, T, 4, 4]), ALU.add))
                first_best(sl, NEXP, down16, wk, oh)
                link(dve.scalar_tensor_tensor(out=sl, in0=oh, scalar=-2 * BIG, in1=sl, op0=ALU.mult, op1=ALU.add))
                first_best(sl, NEXP, down16, wk, ga)
                link(dve.tensor_tensor(ga, ga, oh, ALU.add))
                link(dve.tensor_tensor(ga, ga, sc, ALU.mult))
                link(dve.tensor_reduce(t1, ga, AXX, ALU.add))
                link(dve.reciprocal(t1, t1))
                link(dve.tensor_tensor(ga, ga, bc16(t1), ALU.mult))
                full(dve, ("xT", L, T - 1, 1))
                link(dve.memset(H[:, 0:T * D], 0.0))
                N = 2 * T
                mb = MOE_BASE[L]
                with dve.Fori(0, NEXP // 2) as i:
                    def product(j):
                        b = 2 * (j % 2) + 1
                        dve.wait_ge(bank_full[b], i * T + (mb[b] + j // 2 + 1))
                        dve.wait_ge(bank_free[b - 1], i * T + (mb[b - 1] + j // 2 + 1))
                        tb = 4 + j % 2
                        dve.wait_ge(bank_full[tb], i * T + (mb[tb] + j // 2))
                        dve.tensor_tensor(EX[:, 2 + j % 2, :], PS[:, b, :], EX[:, j % 2, :], ALU.mult)\
                            .then_inc(bank_free[b], 1)

                    def add_up(j):
                        e, t = j // T, j % T
                        dve.wait_ge(bank_free[7], i * N + (mb[7] + j))
                        for hf in range(2):
                            b = 6 + hf
                            dve.wait_ge(bank_full[b], i * N + (mb[b] + j + 1))
                            y = HR[:, t, 512 * hf:512 * hf + 512]
                            ins = dve.scalar_tensor_tensor(out=y, in0=PS[:, b, :],
                                                           scalar=GATE[:, t, bass.ds(2 * i + e, 1)], in1=y,
                                                           op0=ALU.mult, op1=ALU.add).then_inc(bank_free[b], 1)

                    product(0)
                    for j in range(N):
                        if j + 1 < N:
                            product(j + 1)
                        add_up(j)
                ada_copy(L, [10, 11])
                for b in (6, 7):
                    dve.wait_ge(bank_free[b], mb[b] + NEXP * T)
                for c_ in (10, 11):
                    for r in mod_streams(L, c_):
                        read(dve, ("mod", L, c_, r))
                for t in range(T):
                    link(dve.tensor_tensor(HR[:, t, :], HR[:, t, :], GT[:, t // 2, :], ALU.mult))
                    link(dve.scalar_tensor_tensor(out=X[:, t, :], in0=X[:, t, :], scalar=ALPHA, in1=HR[:, t, :],
                                                  op0=ALU.mult, op1=ALU.add))
                    stats(L, "ln2", t)
                for t in range(T):
                    normalise(L, "ln2", t, S["ln2_done"])
                if L < DEPTH - 1:
                    dve.wait_ge(S["ln2_done"], val("ln2_done", L, T - 1))

        @block.tensor
        def _(pe):
            def claim(key):
                b, n = BANK[key]
                if n > 1:
                    pe.wait_ge(bank_free[b], n - 1)
                return PS[:, b, :], bank_full[b]

            def weights(key):
                s, n = PLACE[key]
                pe.wait_ge(w_full[s], 16 * n)
                return slot(key)

            def spread(L, c_):
                read(pe, ("ada", L, c_))
                for r in mod_streams(L, c_):
                    ps, done = claim(("mod", L, c_, r))
                    a = CAT["sel"][0] + r
                    pe.matmul(ps, C[:, a:a + 1].to_broadcast([P, P]), R4[:, c_ % 2, :], start=True, stop=True)\
                        .then_inc(done, 1)

            def ada(L, cs):
                for n, c_ in enumerate(cs):
                    ps, done = claim(("ada", L, c_))
                    w = weights(("ada", L, c_))
                    pe.matmul(ps[0:32, :], IDENT[0:12, c_:c_ + 1].to_broadcast([12, 32]), BA[:, :],
                              start=True, stop=False)
                    for k in range(KD):
                        a = 32 * (k % 4)
                        mm = pe.matmul(ps[a:a + 32, :], CT[:, k, :], w[:, k, :], start=(0 < k < 4), stop=(k >= 4),
                                       tile_position=(0, a))
                    mm.then_inc(done, 1)
                    if n:
                        spread(L, cs[n - 1])
                spread(L, cs[-1])

            def turn(key, pieces):
                ps, done = claim(key)
                for n, piece in enumerate(pieces):
                    mm = pe.transpose(ps[:, P * n:P * n + P], piece, IDENT)
                mm.then_inc(done, 1)

            for L in range(DEPTH):
                T = tiles(L)
                if L == 0:
                    pe.wait_ge(const_in, 16)
                    pe.wait_ge(cT_ready, 1)
                pe.wait_ge(layer_in, 16 * WF_DMAS * (L + 1))
                ps, done = claim(("ab", L))
                if L:
                    full(pe, ("fU", L - 1, tiles(L - 1) - 1))
                for pr in range(2):
                    for n, m in enumerate(("cc", "sc")):
                        o = P * (2 * pr + n)
                        mm = pe.matmul(ps[:, o:o + P], cst(m), WF[:, pr, :], start=True, stop=True)
                mm.then_inc(done, 1)
                turn(("swT", L), [SWR[:, g, :] for g in range(4)])
                pe.wait_ge(layer_small_in, 16 * LAYER_DMAS * (L + 1))
                ada(L, [0, 1, 2, 3])
                for t in range(4):
                    pe.wait_ge(S["h1_ready"], val("h1_ready", L, t))
                    for hf in range(2):
                        turn(("hT", L, t, hf), [HR[:, t, 512 * hf + P * k:512 * hf + P * k + P] for k in range(4)])

                def project(name, c0, cw, n):
                    w = weights(("in", L, name))
                    for t in range(n(L)):
                        for hf in range(2):
                            read(pe, ("hT", L, t, hf))
                        ps, done = claim((name, L, t))
                        for k in range(KD):
                            mm = pe.matmul(ps[:, 0:cw], XT[:, k, P * t:P * t + P], w[:, k, :],
                                           start=(k == 0), stop=(k == KD - 1))
                        mm.then_inc(done, 1)

                for ch in CHUNKS[:4]:
                    project(*ch)
                for t in range(T):
                    read(pe, ("q", L, t))
                    if t < 2:
                        pe.wait_ge(S["q_rot"], val("q_rot", L, t))
                    turn(("qT", L, t), [QR[:, t, P * h:P * h + P] for h in range(HEADS)])
                for t in range(4):
                    read(pe, ("k", L, t))
                    if t < 2:
                        pe.wait_ge(S["k_rot"], val("k_rot", L, t))
                    turn(("kT", L, t), [KR[:, t, P * h:P * h + P] for h in range(HEADS)])
                for t in range(T):
                    read(pe, ("f", L, t))
                    turn(("fT", L, t), [FR[:, t, P * a:P * a + P] for a in range(2)])
                project(*CHUNKS[4])
                read(pe, ("ab", L))
                for t in range(T):
                    read(pe, ("fT", L, t))
                    ps, done = claim(("fU", L, t))
                    for pr in range(2):
                        mm = pe.matmul(ps[:, 256 * pr:256 * pr + 256], FT[:, t, pr, :],
                                       AB[:, pr, :, :].rearrange("p b c -> p (b c)"), start=True, stop=True)
                    mm.then_inc(done, 1)
                for s in range(T // 2):
                    for t in (2 * s, 2 * s + 1):
                        read(pe, ("fU", L, t))
                    for pr in range(2):
                        ps, done = claim(("fY", L, s, pr))
                        for n in range(4):
                            kt, m = n // 2, n % 2
                            a = CAT[("cn", "sn")[m]][0] + SEQ * kt
                            mm = pe.matmul(ps[:, 0:SEQ], U[:, 2 * s + kt, pr, m, :], C[:, a:a + SEQ],
                                           start=(n == 0), stop=(n == 3))
                        mm.then_inc(done, 1)
                read(pe, ("swT", L))
                for t in range(T):
                    pe.wait_ge(S["sguv_ready"], val("sguv_ready", L, t))
                    ps, done = claim(("sg", L, t))
                    for g in range(4):
                        mm = pe.matmul(ps[:, 64 * g:64 * g + 64], SWT[:, g, :], GR[:, t, 256 + 64 * g:320 + 64 * g],
                                       start=True, stop=True)
                    mm.then_inc(done, 1)
                UN = units(L)
                for t in range(4):
                    read(pe, ("kT", L, t))

                def scores(u):
                    t, h = UN[u]
                    read(pe, ("qT", L, t))
                    k0 = 0 if t < 2 else 256
                    for cc in range(2):
                        ps, done = claim(("s", L, u, cc))
                        pe.matmul(ps[:, 0:512 - k0], QT[:, cc, h, P * t:P * t + P], KTv[:, h, k0:512],
                                  start=True, stop=True).then_inc(done, 1)

                scores(0)
                for u, (t, h) in enumerate(UN):
                    if u + 1 < len(UN):
                        scores(u + 1)
                    k0 = 0 if t < 2 else 2
                    pe.wait_ge(S["a_ready"], val("a_ready", L, u))
                    turn(("aT", L, u), [EX[:, 2 * (u % 2), P * n:P * n + P] for n in range(4 - k0)])
                    read(pe, ("aT", L, u))
                    if u == 0:
                        for n in range(4):
                            read(pe, ("v", L, n))
                    ps, done = claim(("pv", L, u))
                    for n in range(4 - k0):
                        mm = pe.matmul(ps[:, 0:P], AT[:, u % 2, P * n:P * n + P], VR[:, k0 + n, P * h:P * h + P],
                                       start=(n == 0), stop=(n == 3 - k0))
                    mm.then_inc(done, 1)
                for t in range(T):
                    pe.wait_ge(S["sgu_ready"], val("sgu_ready", L, t))
                    turn(("gT", L, t), [GR[:, t, P * a:P * a + P] for a in range(2)])
                for t in range(T):
                    pe.wait_ge(S["on_ready"], val("on_ready", L, t))
                    turn(("mT", L, t), [OB[:, t, P * h:P * h + P] for h in range(HEADS)])
                ada(L, [4, 5])
                for s in range(T // 2):
                    for pr in range(2):
                        read(pe, ("fY", L, s, pr))
                for hf in range(2):
                    w = weights(("out", L, hf))
                    for t in range(T):
                        read(pe, ("gT", L, t))
                        read(pe, ("mT", L, t))
                        ps, done = claim(("o", L, hf, t))
                        for k in range(KD):
                            mm = pe.matmul(ps, XT[:, k, P * t:P * t + P], w[:, k, :],
                                           start=(k == 0), stop=(k == KD - 1))
                        mm.then_inc(done, 1)
                ada(L, [6, 7, 8, 9])
                for t in range(T):
                    pe.wait_ge(S["hx_ready"], val("hx_ready", L, t))
                    for hf in range(2):
                        turn(("xT", L, t, hf), [HR[:, t, 512 * hf + P * k:512 * hf + P * k + P] for k in range(4)])
                if L == 0:
                    pe.wait_ge(router_in, 32)
                for t in range(T):
                    for hf in range(2):
                        read(pe, ("xT", L, t, hf))
                    ps, done = claim(("rt", L, t))
                    for k in range(KD):
                        mm = pe.matmul(ps[:, 0:NEXP], XT[:, k, P * t:P * t + P], WR[:, k, :],
                                       start=(k == 0), stop=(k == KD - 1))
                    mm.then_inc(done, 1)
                N = 2 * T
                mb = MOE_BASE[L]
                rb = RING_BASE[L]
                for b in range(8):
                    pe.wait_ge(bank_free[b], mb[b])
                with pe.Fori(0, NEXP // 2) as i:
                    def up(j):
                        e, t = j // T, j % T
                        for n in range(2):
                            s, b = 3 * e + n, 2 * (j % 2) + n
                            if t == 0:
                                pe.wait_ge(w_full[s], i * 16 + 16 * (rb[s] + 1))
                            pe.wait_ge(bank_free[b], i * T + (mb[b] + j // 2))
                            for k in range(KD):
                                mm = pe.matmul(PS[:, b, :], XT[:, k, P * t:P * t + P], moe_up(s)[:, k, :],
                                               start=(k == 0), stop=(k == KD - 1))
                            mm.then_inc(bank_full[b], 1)

                    def down(j):
                        e, t = j // T, j % T
                        b = 4 + j % 2
                        ab = 2 * (j % 2) + 1
                        pe.wait_ge(bank_free[ab], i * T + (mb[ab] + j // 2 + 1))
                        pe.wait_ge(bank_free[b], i * T + (mb[b] + j // 2))
                        for n in range(FE // P):
                            mm = pe.transpose(PS[:, b, P * n:P * n + P], EX[:, 2 + j % 2, P * n:P * n + P], IDENT)
                        mm.then_inc(bank_full[b], 1)
                        s = 3 * e + 2
                        if t == 0:
                            pe.wait_ge(w_full[s], i * 16 + 16 * (rb[s] + 1))
                        pe.wait_ge(bank_free[b], i * T + (mb[b] + j // 2 + 1))
                        for hf in range(2):
                            pe.wait_ge(bank_free[6 + hf], i * N + (mb[6 + hf] + j))
                            for k in range(FE // P):
                                mm = pe.matmul(PS[:, 6 + hf, :], AT[:, j % 2, P * k:P * k + P],
                                               moe_down(s)[:, k, 512 * hf:512 * hf + 512],
                                               start=(k == 0), stop=(k == FE // P - 1))
                            mm.then_inc(bank_full[6 + hf], 1)

                    up(0)
                    for j in range(N):
                        if j + 1 < N:
                            up(j + 1)
                        down(j)
                ada(L, [10, 11])


_INS = ["x", "c", "ctx", "c_ctx", "w_ada", "b_ada", "w_in", "w_fourier", "diff_lambda", "diff_subln", "sgu_ln_g",
        "sgu_ln_b", "sgu_w", "sgu_b", "w_out", "ln_g", "ln_b", "w_router", "router_bias", "moe_w1", "moe_w3", "moe_w2"]


def kernel(**inputs):
    import numpy as _np
    import concourse.bacc as _bacc
    from concourse import mybir as _mybir
    from concourse.bass_utils import run_bass_kernel_spmd as _run

    nc = _bacc.Bacc("TRN2", target_bir_lowering=False, num_devices=1, dynamic_dma_scratch_size=8192)
    arrays, args = {}, []
    for name in _INS:
        a = _np.ascontiguousarray(inputs[name])
        arrays[f"in_{name}"] = a
        args.append(nc.dram_tensor(f"in_{name}", a.shape, _mybir.dt.from_np(a.dtype), kind="ExternalInput").ap())
    table = constants()[0]
    arrays["in_const"] = table
    args.append(nc.dram_tensor("in_const", table.shape, _mybir.dt.float32, kind="ExternalInput").ap())
    args.append(nc.dram_tensor("out_0", (1, SEQ, D), _mybir.dt.float32, kind="ExternalOutput").ap())
    backbone(nc, *args)
    r = _run(nc, [arrays], core_ids=[0])
    return r.results[0]["out_0"]
```

```python
import math
from contextlib import ExitStack

import numpy as np

import concourse.bass as bass
from concourse import mybir

F32 = mybir.dt.float32
I32 = mybir.dt.int32
BF16 = mybir.dt.bfloat16
ALU = mybir.AluOpType
ACT = mybir.ActivationFunctionType
AXX = mybir.AxisListType.X

P = 128
D = 1024
KD = D // P
DEPTH = 2
SEQ = 256
GRID_W = 64
HEADS = 4
DH = 64
NEXP = 16
FE = 512
LN_EPS = 1e-5
ALPHA = float((2 * DEPTH) ** 0.25)
SLOTS = 6
SCALE = DH ** -0.5
BIG = 1e30
CAP = 4 * P
SPILL = 13
PAIRS = NEXP // 2
PER = (2, 1, 2, 1, 2, 2, 2, 2)


def tiles(L):
    return 4 if L < DEPTH - 1 else 2


CHUNKS = [("q", 256, 512, tiles), ("k", 768, 512, lambda L: 4), ("g", 1792, 512, tiles),
          ("f", 0, 256, tiles), ("v", 1280, 512, lambda L: 4)]


def units(L):
    return [(t, h) for t in range(tiles(L)) for h in range(HEADS)]


def mod_streams(L, c):
    return (0, 1) if tiles(L) == 4 or c < 4 else (0,)


COUNTS = {
    "h1_ready": lambda L: 4,
    "q_rot": lambda L: 2, "k_rot": lambda L: 2,
    "pad_zero": lambda L: 1,
    "sguv_ready": tiles, "sgu_ready": tiles,
    "bias_ready": lambda L: len(units(L)), "a_ready": lambda L: len(units(L)),
    "on_ready": tiles,
    "var_ready": lambda L: 4 * tiles(L), "rstd_ready": lambda L: 4 * tiles(L),
    "ln1_done": tiles, "hx_ready": tiles, "ln2_done": tiles,
    "pick_ready": lambda L: NEXP // 4, "mask_ready": lambda L: 1,
    "dest_ready": lambda L: 1, "mixed_ready": tiles,
    "ln1_scaled": tiles, "ln2_scaled": tiles, "h1_scaled": lambda L: 4, "hx_scaled": tiles,
}


def val(name, L, i):
    return sum(COUNTS[name](l) for l in range(L)) + i + 1


def norm_steps(T, kind):
    if kind == "ln1":
        return [(step, t) for t in range(T) for step in "ABC"]
    out = []
    for n in range(T + 2):
        out += [("A", n)] * (n < T) + [("B", n - 1)] * (0 <= n - 1 < T) + [("C", n - 2)] * (n >= 2)
    return out


def first_jobs(L):
    T = tiles(L)
    h = lambda t: [("hT", L, t)]
    if L == 0:
        out = h(0) + h(1) + [("q", L, 0)] + h(2) + [("q", L, 1)] + h(3)
    else:
        out = h(0) + [("q", L, 0)] + h(1) + [("k", L, 0)] + h(2) + [("q", L, 1), ("skip", 2)] + h(3)
    done = set(out)
    return out + [(name, L, t) for name, n in (("q", T), ("k", 4)) for t in range(n) if (name, L, t) not in done]


def plan_layer(L):
    T = tiles(L)

    def ada(cs, L=L):
        out = []
        for n, c in enumerate(cs):
            out.append(("ada", L, c))
            if n:
                out += [("mod", L, cs[n - 1], r) for r in mod_streams(L, cs[n - 1])]
        return out + [("mod", L, cs[-1], r) for r in mod_streams(L, cs[-1])]

    jobs = ada([0, 1, 2, 3]) if L == 0 else []
    jobs += [("ab", L), ("swT", L)]
    for job in first_jobs(L):
        jobs += [job + (hf,) for hf in range(2)] if job[0] == "hT" else [job]
    for name, _, _, n in CHUNKS[2:4]:
        jobs += [(name, L, t) for t in range(n(L))]
    jobs += [("qT", L, t) for t in range(T)] + [("kT", L, t) for t in range(4)]
    jobs += [("fT", L, t) for t in range(T)]
    jobs += [("v", L, t) for t in range(4)]
    jobs += [("fU", L, t) for t in range(T)]
    jobs += [("fY", L, s, pr) for s in range(T // 2) for pr in range(2)]
    jobs += [("sg", L, t) for t in range(T)]
    U = len(units(L))
    jobs += [("s", L, u, c) for u in range(2) for c in range(2)]
    for u in range(U):
        if u + 2 < U:
            jobs += [("s", L, u + 2, 0), ("s", L, u + 2, 1)]
        jobs += [("aT", L, u)] + [("pv", L, u - 1)] * (u > 0)
    jobs += [("pv", L, U - 1)]
    jobs += [("gT", L, t) for t in range(T)] + [("mT", L, t) for t in range(T)]
    jobs += ada([4, 5, 6, 7, 8, 9])
    jobs += [("o", L, hf, 0) for hf in range(2)]
    for t in range(T):
        if t + 1 < T:
            jobs += [("o", L, hf, t + 1) for hf in range(2)]
        else:
            jobs += ada([10, 11])
        jobs += [("xT", L, t, hf) for hf in range(2)] + [("rt", L, t - 1)] * (t > 0)
    jobs += [("rt", L, T - 1)]
    if L + 1 < DEPTH:
        jobs += ada([0], L + 1)
    jobs += [("rk", L, t) for t in range(T)] + [("ct", L)]
    if L + 1 < DEPTH:
        jobs += ada([1], L + 1)
    jobs += [("ix", L)]
    if L + 1 < DEPTH:
        jobs += ada([2, 3], L + 1)
    jobs += [("moe", L)]
    return jobs


def make_plan():
    fills = [0] * 8
    bank, moe_base = {}, {}
    n = 0
    for L in range(DEPTH):
        for key in plan_layer(L):
            if key[0] == "skip":
                n += key[1]
                continue
            if key[0] == "moe":
                moe_base[L] = list(fills)
                for b in range(8):
                    fills[b] += PAIRS * PER[b] + (b in (4, 5))
                continue
            b = n % 8
            n += 1
            fills[b] += 1
            bank[key] = (b, fills[b])
    return bank, moe_base


def ring_plan():
    order, fill = [], [0] * SLOTS
    place, base = {}, {}
    pos = 0

    def put(key):
        nonlocal pos
        s = pos % SLOTS
        pos += 1
        fill[s] += 1
        place[key] = (s, fill[s])
        order.append(key)

    for L in range(DEPTH):
        if L == 0:
            for c in range(4):
                put(("ada", L, c))
        for name, *_ in CHUNKS:
            put(("in", L, name))
        for c in range(4, 10):
            put(("ada", L, c))
        put(("out", L, 0)), put(("out", L, 1))
        put(("ada", L, 10)), put(("ada", L, 11))
        for c in range(4 if L + 1 < DEPTH else 0):
            put(("ada", L + 1, c))
        pos = -(-pos // SLOTS) * SLOTS
        base[L] = list(fill)
        order.append(("moe", L))
        for s in range(SLOTS):
            fill[s] += NEXP // 2
    return order, place, base


def constants():
    n = np.arange(SEQ)
    ang = 2 * np.pi * np.outer(n, n) / SEQ
    norm = 1.0 / math.sqrt(SEQ * DH)
    cn, sn = np.cos(ang) * norm, -np.sin(ang) * norm
    m = np.arange(DH)
    a64 = 2 * np.pi * np.outer(m, m) / DH
    blk = lambda w: np.kron(np.eye(2), w)
    half = DH // 2
    inv = (10000.0 ** (-np.arange(0, half, 2, dtype=np.float32) / half)).astype(np.float32)
    row = np.repeat(np.arange(SEQ // GRID_W, dtype=np.float32), GRID_W)
    col = np.tile(np.arange(GRID_W, dtype=np.float32), SEQ // GRID_W)
    an = np.stack([row[:, None] * inv, col[:, None] * inv], 1).astype(np.float64)
    cos, sin = np.cos(an), np.sin(an)
    rc = np.stack([cos, cos], 2).reshape(SEQ, DH)
    rs = np.stack([-sin, sin], 2).reshape(SEQ, DH)
    two = lambda w: w.reshape(2, P, -1).transpose(1, 0, 2).reshape(P, -1)
    sel = np.zeros((P, 2))
    for j in range(4):
        for r in range(2):
            sel[32 * j + r, r] = 1
    parts = {"ident": np.eye(P), "cn": two(cn), "sn": two(sn), "cc": blk(np.cos(a64)), "sc": blk(np.sin(a64)),
             "rc": two(rc), "rs": two(rs), "sel": sel,
             "down16": np.tile(np.arange(16, 0, -1), (P, 1)), "down4": np.tile(np.arange(4, 0, -1), (P, 1)),
             "iota": np.tile(np.arange(CAP), (P, 1)), "before": np.triu(np.ones((P, P)), 1), "one": np.ones((P, 1)),
             "token": np.arange(CAP).reshape(4, P).T,
             "token2": np.stack([np.tile(np.arange(P)[:, None], (1, 4)), np.tile(P * np.arange(4), (P, 1))],
                                2).reshape(P, 8),
             "zero": np.zeros((P, 1))}
    at, cols, o = {}, [], 0
    for k, v in parts.items():
        at[k] = (o, o + v.shape[1])
        o += v.shape[1]
        cols.append(v)
    return np.concatenate(cols, 1).astype(np.float32), at


def backbone(nc, x, c, ctx, c_ctx, w_ada, b_ada, w_in, w_fourier, diff_lambda, diff_subln, sgu_ln_g, sgu_ln_b,
             sgu_w, sgu_b, w_out, ln_g, ln_b, w_router, router_bias, moe_w1, moe_w3, moe_w2, const, out):
    CAT = constants()[1]
    BANK, MOE_BASE = make_plan()
    RING, PLACE, RING_BASE = ring_plan()
    NCONST = const.shape[1]
    LAM_INIT = [0.8 - 0.6 * math.exp(-0.3 * l) for l in range(DEPTH)]

    es = ExitStack()
    with es:
        def sb(name, shape):
            return es.enter_context(nc.sbuf_tensor(name, shape, F32))

        def sem(name):
            return es.enter_context(nc.semaphore(name))

        X = sb("X", [P, 4, D])
        H = sb("H", [P, 4 * D])
        XT = sb("XT", [P, KD, 512])
        RA = sb("RA", [P, 2048])
        RB = sb("RB", [P, 2048])
        RC = sb("RC", [P, 2048])
        KT = sb("KT", [P, 2048])
        EX = sb("EX", [P, 4, 512])
        AT = sb("AT", [P, 2, 512])
        W = sb("W", [P, SLOTS, 4096])
        R4 = sb("R4", [P, 2, 512])
        CT = sb("CT", [P, KD, 32])
        CR = sb("CR", [P, 2, KD])
        CE = sb("CE", [P, 2, KD])
        C = sb("C", [P, NCONST])
        BA = sb("BA", [12 * DEPTH, 512])
        WF = sb("WF", [P, 2, P])
        AB = sb("AB", [P, 2, 2, P])
        SWT = sb("SWT", [P, 4, P])
        LM = sb("LM", [P, 4, DH])
        GAIN = sb("GAIN", [P, P])
        SG = sb("SG", [P, 2, 256])
        SB_ = sb("SB_", [P, 4])
        WR = sb("WR", [P, KD, NEXP])
        RBIAS = sb("RBIAS", [P, NEXP])
        JUNK = sb("JUNK", [P, P])
        ST = sb("ST", [P, 2, 6])
        MV = sb("MV", [P, 4, 2])
        VAR = sb("VAR", [P, 24, 4])
        RSTD = sb("RSTD", [P, 24, 4])
        HALF = sb("HALF", [P, 4])
        LAM = sb("LAM", [P, 8])
        MX = sb("MX", [P, 2, 2])
        NB = sb("NB", [P, 2, 2])
        SM = sb("SM", [P, 2, 2])
        RI = sb("RI", [P, 2, 2])
        SS = sb("SS", [P, 4, HEADS])
        ER = sb("ER", [P, 4, NEXP])
        SCO = sb("SCO", [P, 4, NEXP])
        SEL = sb("SEL", [P, 4, NEXP])
        WK = sb("WK", [P, 4, NEXP])
        OH = sb("OH", [P, 4, NEXP])
        GATE = sb("GATE", [P, 4, NEXP])
        PG = sb("PG", [P, 4, 6, 4])
        GS = sb("GS", [P, 4, 4])
        GM = sb("GM", [P, 4, 4])
        T1 = sb("T1", [P, 4, 1])
        OH2 = sb("OH2", [P, 4, NEXP])
        POS = sb("POS", [P, 4, NEXP])
        POSM = sb("POSM", [P, 4, NEXP])
        WK2 = sb("WK2", [P, 4, 2])
        DF = sb("DF", [P, 4, 2])
        CNT = sb("CNT", [P, 5, 17])
        IDX = es.enter_context(nc.sbuf_tensor("IDX", [P, 20], I32))
        IOTA16 = es.enter_context(nc.sbuf_tensor("IOTA16", [P, P], BF16))
        POS16 = es.enter_context(nc.sbuf_tensor("POS16", [P, 4, NEXP], BF16))
        TOKEN16 = es.enter_context(nc.sbuf_tensor("TOKEN16", [P, 4, 2], BF16))
        IXS = es.enter_context(nc.sbuf_tensor("IXS", [P, 2], I32))
        IXO = es.enter_context(nc.sbuf_tensor("IXO", [P, 1], I32))
        DEST = es.enter_context(nc.sbuf_tensor("DEST", [P, 4, 2], I32))
        META = es.enter_context(nc.sbuf_tensor("META", [1, DEPTH, 3, 17], I32))
        hx_rows = nc.dram_tensor("hx_rows", (CAP, D), F32).ap()
        y_rows = nc.dram_tensor("y_rows", (3 * CAP, D), F32).ap()
        PS = es.enter_context(nc.psum_tensor("PS", [P, 8, 512], F32))

        def cst(name):
            a, b = CAT[name]
            return C[:, a:b]

        IDENT = cst("ident")
        SH = RA[:, :].rearrange("p (s d) -> p s d", s=2)
        SCL = RB[:, :].rearrange("p (s d) -> p s d", s=2)
        GT = RC[:, :].rearrange("p (s d) -> p s d", s=2)
        VEC = [SH, SCL, GT, SH, SCL, GT]
        HR = H[:, :].rearrange("p (t d) -> p t d", t=4)
        QT = H[:, :].rearrange("p (c h t) -> p c h t", c=2, h=HEADS)
        QR = RA[:, :].rearrange("p (t d) -> p t d", t=4)
        VR = QR
        KR = RB[:, :].rearrange("p (t d) -> p t d", t=4)
        FT = RB[:, 0:1024].rearrange("p (t a c) -> p t a c", t=4, a=2)
        OB = KR
        GR = RC[:, :].rearrange("p (t d) -> p t d", t=4)
        KTv = KT[:, :].rearrange("p (h t) -> p h t", h=HEADS)
        LNR = KT[:, :].rearrange("p (a d) -> p a d", a=2)
        FR = AT[:, :, :].rearrange("p a (b d) -> p (a b) d", b=2)
        U = EX[:, :, :].rearrange("p t (a b c) -> p t a b c", a=2, b=2)
        XG = H[:, 0:2048].rearrange("p (b d) -> p b d", b=2)
        YO = H[:, 2048:4096].rearrange("p (b d) -> p b d", b=2)
        PB = XT[:, :, :].rearrange("p k n -> p (k n)").bitcast(BF16).rearrange("p (g t s) -> p g t s", g=4, t=4)
        XGT = XT[:, 0:4, :].rearrange("p (b k) (c s) -> p b (k c) s", b=2, c=4)
        XGO = XT[:, 4:6, :].rearrange("p a b -> p (a b)")
        PBO = XT[:, 6, :].rearrange("p (t s) -> p t s", t=4)
        G2 = H[:, :].rearrange("p (b k d) -> p b k d", b=2, k=2)
        SWR = EX[:, 3, :].rearrange("p (g q) -> p g q", g=4)

        bank_full = [sem(f"bank_full{b}") for b in range(8)]
        bank_free = [sem(f"bank_free{b}") for b in range(8)]
        w_full = [sem(f"w_full{s}") for s in range(SLOTS)]
        S = {name: sem(name) for name in COUNTS}
        x_in = sem("x_in")
        const_in = sem("const_in")
        ba_in = sem("ba_in")
        sgu_w_in = sem("sgu_w_in")
        c_in = sem("c_in")
        router_in = sem("router_in")
        layer_in = sem("layer_in")
        layer_small_in = sem("layer_small_in")
        wf_zero = sem("wf_zero")
        ln_in = sem("ln_in")
        lamgain_ready = sem("lamgain_ready")
        setup_ready = sem("setup_ready")
        cexp_ready = sem("cexp_ready")
        cT_ready = sem("cT_ready")
        dve_step = sem("dve_step")
        act_step = sem("act_step")
        pool_step = sem("pool_step")
        out_written = sem("out_written")
        lam_exp = sem("lam_exp")
        lam_sum = sem("lam_sum")
        hx_written = sem("hx_written")
        xg_in = [sem(f"xg_in{b}") for b in range(2)]
        y_written = [sem(f"y_written{b}") for b in range(2)]
        g_in = [sem(f"g_in{b}") for b in range(2)]
        ix_ready = sem("ix_ready")
        spill_rows_in = [sem(f"spill_rows_in{L}") for L in range(DEPTH)]
        spill_written = [sem(f"spill_written{L}") for L in range(DEPTH)]
        spill_step = [sem(f"spill_step{L}") for L in range(DEPTH)]
        LAYER_DMAS = 5
        WF_DMAS = 4

        def full(eng, key):
            b, n = BANK[key]
            eng.wait_ge(bank_full[b], n)
            return PS[:, b, :]

        def freed(key):
            return bank_free[BANK[key][0]]

        passed = sem("passed")

        def wait_apart(eng, semaphore, value):
            eng.wait_ge(semaphore, value)
            eng.sem_inc(passed, 1)

        def read(eng, key):
            b, n = BANK[key]
            eng.wait_ge(bank_free[b], n)

        w_src = {}
        for L in range(DEPTH):
            for n in range(12):
                w_src["ada", L, n] = (w_ada[L, :, 512 * n:512 * n + 512], 512)
            for name, c0, cw, _ in CHUNKS:
                w_src["in", L, name] = (w_in[L, :, c0:c0 + cw], cw)
            for hf in range(2):
                w_src["out", L, hf] = (w_out[L, :, 512 * hf:512 * hf + 512], 512)

        def slot(key):
            s = PLACE[key][0]
            cw = w_src[key][1]
            return W[:, s, 0:KD * cw].rearrange("p (k n) -> p k n", k=KD)

        def moe_up(s):
            return W[:, s, :].rearrange("p (k n) -> p k n", k=KD)

        def moe_down(s):
            return W[:, s, :].rearrange("p (k n) -> p k n", k=FE // P)

        def last_job(key):
            kind, L, n = key
            if kind == "ada":
                return key
            if kind == "in":
                return (n, L, {ch[0]: ch[3] for ch in CHUNKS}[n](L) - 1)
            return ("o", L, n, tiles(L) - 1)

        def req(L, kind, t):
            order = ["sgu", "att", "ln1", "ln2"]
            return sum(4 * tiles(l) for l in range(L)) + order.index(kind) * tiles(L) + t

        block = es.enter_context(nc.Block())

        @block.sync
        def _(sp):
            def moe_load(L, e, n, at):
                s = 3 * e + n
                k = KD if n < 2 else FE // P
                dst = W[:, s, :].rearrange("p (k n) -> p k n", k=k)
                src = (moe_w1, moe_w3, moe_w2)[n][L, at, :, :]
                src = src.rearrange("(k p) n -> p k n", p=P) if isinstance(at, int) else \
                    src.rearrange("o (k p) n -> p (o k) n", p=P)
                sp.dma_start(dst, src).then_inc(w_full[s], 16)

            with nc.allow_non_contiguous_dma("two vectors, as columns"):
                sp.dma_start(CR[:, 0, :], c[0].rearrange("(k p) -> p k", p=P)).then_inc(c_in, 16)
                sp.dma_start(CR[:, 1, :], c_ctx.rearrange("(k p) -> p k", p=P)).then_inc(c_in, 16)
            sp.dma_start(BA[:, :], b_ada.rearrange("l (c n) -> (l c) n", n=512)).then_inc(ba_in, 16)
            sp.dma_start(C[:, :], const).then_inc(const_in, 16)
            last = [None] * SLOTS
            order = [last_job(key) for key in RING if key[0] != "moe"]
            for key in RING:
                if key[0] == "moe":
                    L = key[1]
                    T = tiles(L)
                    mb = MOE_BASE[L]
                    for s in sorted(range(SLOTS), key=lambda s: order.index(last[s])):
                        full(sp, last[s])
                        moe_load(L, s // 3, s % 3, s // 3)
                    sp.wait_ge(spill_step[L], 1)
                    with sp.Fori(1, PAIRS) as i:
                        for e in range(2):
                            spilt = sp.value_load(META[0:1, L, 1, bass.ds(2 * i + (e - 1), 1)], min_val=0, max_val=7)
                            for n in range(3):
                                if n < 2:
                                    b = 2 * e + 1
                                    sp.wait_ge(bank_full[b], i + mb[b])
                                else:
                                    sp.wait_ge(bank_full[7], i * 2 + (mb[7] - 1 + e))
                                if n == 0:
                                    sp.wait_ge(spill_step[L], spilt * SPILL + 1)
                                moe_load(L, e, n, bass.ds(2 * i + e, 1))
                    last = [("moe", L)] * SLOTS
                    continue
                s, n = PLACE[key]
                if last[s] and last[s][0] == "moe":
                    L0 = last[s][1]
                    n_, e_ = s % 3, s // 3
                    mb = MOE_BASE[L0]
                    if n_ < 2:
                        sp.wait_ge(bank_full[2 * e_ + 1], mb[2 * e_ + 1] + PAIRS)
                    else:
                        sp.wait_ge(bank_full[7], mb[7] + 2 * PAIRS - 1 + e_)
                    spilt = sp.value_load(META[0:1, L0, 1, 16:17], min_val=0, max_val=7)
                    sp.wait_ge(spill_step[L0], spilt * SPILL + 1)
                elif last[s]:
                    full(sp, last[s])
                if key == ("in", key[1], "f") and key[1]:
                    for b in range(2):
                        sp.wait_ge(g_in[b], 16 * sum(tiles(l) for l in range(key[1])))
                if key == ("ada", 0, 3):
                    sp.dma_start(X[:, 0:2, :], x[0].rearrange("(t p) d -> p t d", p=P)).then_inc(x_in, 16)
                    sp.dma_start(X[:, 2:4, :], ctx[0].rearrange("(t p) d -> p t d", p=P)).then_inc(x_in, 16)
                sp.dma_start(slot(key), w_src[key][0].rearrange("(k p) n -> p k n", p=P)).then_inc(w_full[s], 16)
                last[s] = last_job(key)

        @block.gpsimd
        def _(pool):
            pool.memset(HALF[:, :], -0.5).then_inc(pool_step, 1)
            pool.wait_ge(pool_step, 1)

            def params(L):
                if L:
                    pool.wait_ge(S["on_ready"], val("on_ready", L - 1, tiles(L - 1) - 1))
                    pool.wait_ge(S["sgu_ready"], val("sgu_ready", L - 1, tiles(L - 1) - 1))
                pool.dma_start(LM[:, :, :].rearrange("p a d -> p (a d)"),
                               diff_lambda[L].rearrange("a d -> (a d)").partition_broadcast(P)).then_inc(layer_small_in, 16)
                pool.dma_start(GAIN[:, :], diff_subln[L].partition_broadcast(P)).then_inc(layer_small_in, 16)
                pool.dma_start(SG[:, 0, :], sgu_ln_g[L].partition_broadcast(P)).then_inc(layer_small_in, 16)
                pool.dma_start(SG[:, 1, :], sgu_ln_b[L].partition_broadcast(P)).then_inc(layer_small_in, 16)
                with nc.allow_non_contiguous_dma("512 words"):
                    pool.dma_start(SB_[:, :], sgu_b[L].rearrange("g q -> q g")).then_inc(layer_small_in, 16)
                if L == 0:
                    pool.wait_ge(wf_zero, 1)
                for g in range(4):
                    o = 64 * (g % 2)
                    pool.dma_start(WF[o:o + 64, g // 2, o:o + 64], w_fourier[L, g]).then_inc(layer_in, 16)

            def load_sgu_w(L):
                if L:
                    pool.wait_ge(bank_full[7], MOE_BASE[L - 1][7] + 2 * PAIRS)
                pool.dma_start(SWR, sgu_w[L].rearrange("g q p -> q g p")).then_inc(sgu_w_in, 16)

            def norm(L, kind, done):
                for step, t in norm_steps(tiles(L), kind):
                    if step == "A":
                        r = req(L, kind, t)
                        pool.wait_ge(S["var_ready"], r + 1)
                        pool.tensor_tensor(RSTD[:, r, 0:1], VAR[:, r, 0:1], HALF[:, 0:1], ALU.pow)\
                            .then_inc(S["rstd_ready"], 1)
                    elif step == "B":
                        name = kind + "_scaled"
                        pool.wait_ge(S[name], val(name, L, t))
                        pool.tensor_tensor(X[:, t, :], X[:, t, :], LNR[:, 1, :], ALU.add).then_inc(done, 1)
                    elif kind == "ln1":
                        shift("hx", L, t)
                    elif L + 1 < DEPTH:
                        shift("h1", L + 1, t)

            def shift(h, L, t):
                pool.wait_ge(S[h + "_scaled"], val(h + "_scaled", L, t))
                pool.tensor_tensor(HR[:, t, :], HR[:, t, :], SH[:, t // 2, :], ALU.add).then_inc(S[h + "_ready"], 1)

            def rstds(L, kind):
                for t in range(tiles(L)):
                    r = req(L, kind, t)
                    n = HEADS if kind == "att" else 1
                    pool.wait_ge(S["var_ready"], r + 1)
                    pool.tensor_tensor(RSTD[:, r, 0:n], VAR[:, r, 0:n], HALF[:, 0:n], ALU.pow).then_inc(S["rstd_ready"], 1)

            def spill_gather(L, before, j):
                wait_apart(pool, spill_step[L], (before + (j - 1)) * SPILL + 4)
                pool.indirect_dma_start(out=XGO, out_offset=None, in_=hx_rows,
                                        in_offset=bass.IndirectOffsetOnAxis(ap=IXO[:, 0:1], axis=0))\
                    .then_inc(spill_rows_in[L], 16)

            def spill_counts(L, i, p):
                return (pool.value_load(META[0:1, L, 0, bass.ds(2 * i + p, 1)], min_val=0, max_val=CAP),
                        pool.value_load(META[0:1, L, 1, bass.ds(2 * i + p, 1)], min_val=0, max_val=7))

            def spill_ahead(L, i, p):
                cnt, before = spill_counts(L, i, p)
                with pool.If(cnt > P):
                    spill_gather(L, before, 1)

            def spill(L, i, p):
                cnt, before = spill_counts(L, i, p)
                with pool.If(cnt > P):
                    with pool.Fori(1, tiles(L)) as j:
                        with pool.If(cnt > j * P):
                            v = (before + (j - 1)) * SPILL + 1
                            wait_apart(pool, spill_step[L], v + 12)
                            first = pool.value_load(META[0:1, L, 2, bass.ds(2 * i + p, 1)], min_val=0, max_val=2 * CAP)
                            pool.dma_start(y_rows[bass.ds(first + j * P, P), :], YO[:, p, :])\
                                .then_inc(spill_written[L], 16)
                            pool.wait_ge(spill_written[L], (before + j) * 16)
                            pool.sem_inc(spill_step[L], 1)
                            wait_apart(pool, spill_step[L], v + SPILL)
                            with pool.If(cnt > (j + 1) * P):
                                spill_gather(L, before, j + 1)
                        with pool.Else():
                            pool.nop()
                    pool.nop()

            def experts(L):
                mb = MOE_BASE[L]
                g0, k0 = 19 * L, (10 * L + 2, 9 * L + 1)
                pool.wait_ge(hx_written, 16 * sum(tiles(l) for l in range(L + 1)))
                read(pool, ("ix", L))

                def gather(p, col, count):
                    pool.tensor_copy(IXS[:, p:p + 1], IDX[:, col]).then_inc(ix_ready, 1)
                    if isinstance(count, int):
                        pool.wait_ge(ix_ready, count)
                    else:
                        wait_apart(pool, ix_ready, count)
                    pool.indirect_dma_start(out=XG[:, p, :], out_offset=None, in_=hx_rows,
                                            in_offset=bass.IndirectOffsetOnAxis(ap=IXS[:, p:p + 1], axis=0))\
                        .then_inc(xg_in[p], 16)

                for p in range(2):
                    gather(p, slice(p, p + 1), g0 + p + 1)

                def next_gather(p, turned, arrived, col, count):
                    pool.wait_ge(bank_full[5], turned)
                    pool.wait_ge(xg_in[p], arrived)
                    gather(p, col, count)

                def rows_out(i, p):
                    for b in (6, 7):
                        pool.wait_ge(bank_free[b], i * 2 + (mb[b] + 1 + p))
                    pool.wait_ge(y_written[1 - p], i * 16 + 16 * (PAIRS * L + 1 + p))
                    first = pool.value_load(META[0:1, L, 2, bass.ds(2 * i + p, 1)], min_val=0, max_val=2 * CAP)
                    pool.dma_start(y_rows[bass.ds(first, P), :], YO[:, p, :]).then_inc(y_written[p], 16)

                if L == 0:
                    pool.wait_ge(const_in, 16)
                    for p in range(2):
                        pool.dma_start(y_rows[0:1, P * p:P * p + P], IDENT[0:1, :]).then_inc(y_written[p], 16)
                        pool.wait_ge(y_written[p], 16)
                next_gather(0, mb[5] + 1, 16 * (10 * L + 1), slice(2, 3), g0 + 3)
                with pool.Fori(0, PAIRS) as i:
                    next_gather(1, i * 2 + (mb[5] + 2), i * 16 + 16 * k0[1], bass.ds(2 * i + 3, 1), i * 2 + (g0 + 4))
                    spill_ahead(L, i, 0)
                    rows_out(i, 0)
                    spill(L, i, 0)
                    next_gather(0, i * 2 + (mb[5] + 3), i * 16 + 16 * k0[0], bass.ds(2 * i + 4, 1), i * 2 + (g0 + 5))
                    spill_ahead(L, i, 1)
                    rows_out(i, 1)
                    spill(L, i, 1)
                for p in range(2):
                    pool.wait_ge(y_written[p], 16 * (PAIRS * (L + 1) + 1))
                    pool.wait_ge(xg_in[p], 16 * (10 - p) * (L + 1))
                pool.wait_ge(S["dest_ready"], val("dest_ready", L, 0))
                full_x17 = mb[5] + 1 + 2 * PAIRS
                pool.wait_ge(bank_full[5], full_x17)
                for t in range(tiles(L)):
                    if t >= 2:
                        pool.wait_ge(S["mixed_ready"], val("mixed_ready", L, t - 2))
                    for k in range(2):
                        pool.indirect_dma_start(out=G2[:, t % 2, k, :], out_offset=None, in_=y_rows[0:2 * P * tiles(L), :],
                                                in_offset=bass.IndirectOffsetOnAxis(ap=DEST[:, t, k:k + 1], axis=0))\
                            .then_inc(g_in[t % 2], 16)

            params(0)
            load_sgu_w(0)
            for L in range(DEPTH):
                if L == 0:
                    for t in range(4):
                        shift("h1", 0, t)
                full(pool, ("hT", L, 3, 1))
                pool.memset(QT[64:128, 0, :, :].rearrange("p h t -> p (h t)"), 0.0).then_inc(pool_step, 1)
                pool.wait_ge(pool_step, L + 2)
                pool.memset(QT[0:64, 1, :, :].rearrange("p h t -> p (h t)"), 0.0).then_inc(S["pad_zero"], 1)
                pool.wait_ge(S["pad_zero"], val("pad_zero", L, 0))
                rstds(L, "sgu")
                rstds(L, "att")
                for j in range(2):
                    if j == 0:
                        full(pool, ("s", L, len(units(L)) - 1, 1))
                    else:
                        pool.wait_ge(S["ln1_done"], val("ln1_done", L, tiles(L) - 1))
                    pool.dma_start(LNR[:, 0, :], ln_g[L, j].partition_broadcast(P)).then_inc(ln_in, 16)
                    pool.dma_start(LNR[:, 1, :], ln_b[L, j].partition_broadcast(P)).then_inc(ln_in, 16)
                    if j == 0:
                        pool.wait_ge(ln_in, 32 * (2 * L + 1))
                        norm(L, "ln1", S["ln1_done"])
                    else:
                        if L + 1 < DEPTH:
                            params(L + 1)
                        experts(L)
                        if L + 1 < DEPTH:
                            load_sgu_w(L + 1)
                        norm(L, "ln2", S["ln2_done"])

        @block.scalar
        def _(act):
            act.wait_ge(const_in, 16)
            act.dma_start(WR[:, :, :], w_router.rearrange("(k p) e -> p k e", p=P)).then_inc(router_in, 16)
            act.dma_start(RBIAS[:, :], router_bias.partition_broadcast(P)).then_inc(router_in, 16)
            act.wait_ge(c_in, 32)
            nc.scalar.activation(CE[:, :, :], CR[:, :, :], ACT.Exp, scale=-1.0).then_inc(cexp_ready, 1)

            def copy(dst, src, done):
                nc.scalar.activation(dst, src, ACT.Copy).then_inc(done, 1)

            def ada_rows(L, cs):
                for n, c_ in enumerate(cs):
                    key = ("ada", L, c_)
                    ps = full(act, key)
                    pc, pL = (c_ - 2, L) if c_ >= 2 else (c_ + 10, L - 1)
                    full(act, ("mod", pL, pc, mod_streams(pL, pc)[-1]))
                    copy(R4[:, c_ % 2, :], ps, freed(key))
                    if n:
                        mods(L, [cs[n - 1]])
                mods(L, [cs[-1]])

            def mods(L, cs):
                for c_ in cs:
                    for r in mod_streams(L, c_):
                        v, hf = c_ // 2, c_ % 2
                        key = ("mod", L, c_, r)
                        ps = full(act, key)
                        if v == 0 and L and hf == 0 and r == 0:
                            act.wait_ge(S["hx_ready"], val("hx_ready", L - 1, tiles(L - 1) - 1))
                        if v == 5 and hf == 0 and r == 0:
                            act.wait_ge(S["ln1_done"], val("ln1_done", L, tiles(L) - 1))
                        copy(VEC[v][:, r, 512 * hf:512 * hf + 512], ps, freed(key))

            def lambdas(L):
                act.wait_ge(lam_sum, L + 1)
                nc.scalar.activation(LAM[:, 2:4], LAM[:, 0:2], ACT.Exp).then_inc(lam_exp, 1)

            mods(0, [0, 1, 2, 3])
            for L in range(DEPTH):
                T = tiles(L)
                for t in range(4):
                    for hf in range(2):
                        key = ("hT", L, t, hf)
                        ps = full(act, key)
                        copy(XT[:, 4 * hf:4 * hf + 4, P * t:P * t + P], ps.rearrange("p (k t) -> p k t", k=4), freed(key))
                if L == 0:
                    lambdas(0)
                act.wait_ge(S["h1_ready"], val("h1_ready", L, 3))
                for key in first_jobs(L):
                    if key[0] in ("q", "k"):
                        copy((QR if key[0] == "q" else KR)[:, key[2], :], full(act, key), freed(key))
                for t in range(T):
                    key = ("g", L, t)
                    ps = full(act, key)
                    nc.scalar.activation(GR[:, t, :], ps, ACT.Gelu_apprx_tanh)\
                        .then_inc(freed(key), 1)
                for t in range(T):
                    key = ("f", L, t)
                    copy(FR[:, t, :], full(act, key)[:, 0:256], freed(key))
                act.wait_ge(S["pad_zero"], val("pad_zero", L, 0))
                for t in range(T):
                    key = ("qT", L, t)
                    ps = full(act, key).rearrange("p (h t) -> p h t", h=HEADS)
                    for cc in range(2):
                        a = 64 * cc
                        ins = nc.scalar.activation(QT[a:a + 64, cc, :, P * t:P * t + P], ps[a:a + 64], ACT.Copy)
                    ins.then_inc(freed(key), 1)
                for t in range(T):
                    key = ("fT", L, t)
                    copy(FT[:, t, :, :], full(act, key)[:, 0:256].rearrange("p (a c) -> p a c", a=2), freed(key))
                for t in range(4):
                    key = ("v", L, t)
                    copy(VR[:, t, :], full(act, key), freed(key))
                for s in range(T // 2):
                    for pr in range(2):
                        key = ("fY", L, s, pr)
                        copy(XT[:, pr, SEQ * s:SEQ * s + SEQ], full(act, key)[:, 0:SEQ], freed(key))
                UN = units(L)

                def exps(u):
                    t, h = UN[u]
                    nk = 512 if t < 2 else 256
                    act.wait_ge(S["bias_ready"], val("bias_ready", L, u))
                    if u >= 2:
                        full(act, ("aT", L, u - 2))
                    for cc in range(2):
                        key = ("s", L, u, cc)
                        ps = full(act, key)
                        ins = nc.scalar.activation(EX[:, 2 * (u % 2) + cc, 0:nk], ps[:, 0:nk], ACT.Exp,
                                                   bias=NB[:, u % 2, cc:cc + 1], scale=SCALE,
                                                   accum_out=SM[:, u % 2, cc:cc + 1]).then_inc(freed(key), 1)

                def turned_out(u):
                    t, h = UN[u]
                    nk = 512 if t < 2 else 256
                    key = ("aT", L, u)
                    ps = full(act, key)
                    if u >= 2:
                        full(act, ("pv", L, u - 2))
                    copy(AT[:, u % 2, 0:nk], ps[:, 0:nk], freed(key))

                def results_out(u):
                    t, h = UN[u]
                    key = ("pv", L, u)
                    ps = full(act, key)
                    nc.scalar.activation(OB[:, t, P * h:P * h + P], ps[:, 0:P], ACT.Copy)
                    if u:
                        read(act, ("pv", L, u - 1))
                    nc.scalar.activation(JUNK[:, :], ps[:, 0:P], ACT.Square, accum_out=SS[:, t, h:h + 1])\
                        .then_inc(freed(key), 1)

                exps(0)
                for u in range(len(UN)):
                    if u + 1 < len(UN):
                        exps(u + 1)
                    turned_out(u)
                    if u:
                        results_out(u - 1)
                results_out(len(UN) - 1)
                for t in range(T):
                    key = ("gT", L, t)
                    copy(XT[:, 6:8, P * t:P * t + P], full(act, key)[:, 0:256].rearrange("p (k t) -> p k t", k=2), freed(key))
                for t in range(T):
                    key = ("mT", L, t)
                    copy(XT[:, 2:6, P * t:P * t + P], full(act, key).rearrange("p (k t) -> p k t", k=4), freed(key))
                mods(L, [4, 5, 6, 7, 8, 9])
                def router_exp(t):
                    key = ("rt", L, t)
                    ps = full(act, key)
                    nc.scalar.activation(ER[:, t, :], ps[:, 0:NEXP], ACT.Exp, scale=-1.0)\
                        .then_inc(freed(key), 1)

                for t in range(T):
                    if t == T - 1:
                        ada_rows(L, [10, 11])
                    for hf in range(2):
                        key = ("xT", L, t, hf)
                        copy(XT[:, 4 * hf:4 * hf + 4, P * t:P * t + P],
                             full(act, key).rearrange("p (k t) -> p k t", k=4), freed(key))
                    act.dma_start(hx_rows[P * t:P * t + P, :], HR[:, t, :]).then_inc(hx_written, 16)
                    if t:
                        router_exp(t - 1)
                router_exp(T - 1)
                if L + 1 < DEPTH:
                    for cs in ([0], [1], [2, 3]):
                        ada_rows(L + 1, cs)
                mb = MOE_BASE[L]

                def rows_turned(p, n4, n5):
                    for hf, n in ((0, n4), (1, n5)):
                        act.wait_ge(bank_full[4 + hf], n)
                        nc.scalar.activation(XGT[:, p, 4 * hf:4 * hf + 4, :],
                                             PS[:, 4 + hf, :].rearrange("p (k s) -> p k s", k=4), ACT.Copy)\
                            .then_inc(bank_free[4 + hf], 1)

                def spill(i, p):
                    cnt = act.value_load(META[0:1, L, 0, bass.ds(2 * i + p, 1)], min_val=0, max_val=CAP)
                    before = act.value_load(META[0:1, L, 1, bass.ds(2 * i + p, 1)], min_val=0, max_val=7)
                    step = spill_step[L]
                    with act.If(cnt > P):
                        with act.Fori(1, T) as j:
                            with act.If(cnt > j * P):
                                v = (before + (j - 1)) * SPILL + 1
                                act.wait_ge(step, v + 4)
                                for hf in range(2):
                                    ins = nc.scalar.activation(XGT[:, p, 4 * hf:4 * hf + 4, :],
                                                               PS[:, 4 + hf, :].rearrange("p (k s) -> p k s", k=4),
                                                               ACT.Copy)
                                ins.then_inc(step, 1)
                                act.wait_ge(step, v + 6)
                                nc.scalar.activation(EX[:, p, :], PS[:, 2 * p, :], ACT.Silu).then_inc(step, 1)
                                act.wait_ge(step, v + 9)
                                nc.scalar.activation(AT[:, p, :], PS[:, 2 * p, :], ACT.Copy).then_inc(step, 1)
                                wait_apart(act, step, v + SPILL)
                            with act.Else():
                                act.nop()
                        act.nop()

                act.wait_ge(spill_step[L], 1)
                rows_turned(0, mb[4] + 1, mb[5] + 1)
                with act.Fori(0, PAIRS) as i:
                    def silu(p):
                        b = 2 * p
                        act.wait_ge(bank_full[b], i * 2 + (mb[b] + 1))
                        act.wait_ge(bank_free[b + 1], i + mb[b + 1])
                        nc.scalar.activation(EX[:, p, :], PS[:, b, :], ACT.Silu).then_inc(bank_free[b], 1)

                    def turned(p):
                        b = 2 * p
                        act.wait_ge(bank_full[b], i * 2 + (mb[b] + 2))
                        act.wait_ge(bank_full[7], i * 2 + (mb[7] - 1 + p))
                        nc.scalar.activation(AT[:, p, :], PS[:, b, :], ACT.Copy).then_inc(bank_free[b], 1)

                    def result(p):
                        act.wait_ge(bank_full[6], i * 2 + (mb[6] + 1 + p))
                        act.wait_ge(y_written[p], i * 16 + 16 * (PAIRS * L + 1))
                        nc.scalar.activation(YO[:, p, 0:512], PS[:, 6, :], ACT.Copy).then_inc(bank_free[6], 1)

                    silu(0)
                    rows_turned(1, i * 2 + (mb[4] + 2), i * 2 + (mb[5] + 2))
                    silu(1)
                    turned(0)
                    result(0)
                    spill(i, 0)
                    rows_turned(0, i * 2 + (mb[4] + 3), i * 2 + (mb[5] + 3))
                    turned(1)
                    result(1)
                    spill(i, 1)
                if L + 1 < DEPTH:
                    lambdas(L + 1)
            for t in range(2):
                act.wait_ge(S["ln2_done"], val("ln2_done", DEPTH - 1, t))
                act.dma_start(out[0, P * t:P * t + P, :], X[:, t, :]).then_inc(out_written, 16)
            act.wait_ge(out_written, 32)

        @block.vector
        def _(dve):
            steps = [0]

            def link(ins):
                steps[0] += 1
                ins.then_inc(dve_step, 1)
                dve.wait_ge(dve_step, steps[0])

            dve.memset(WF[:, :, :].rearrange("p a b -> p (a b)"), 0.0).then_inc(wf_zero, 1)
            link(dve.memset(CT[:, :, :].rearrange("p a b -> p (a b)"), 0.0))
            dve.wait_ge(c_in, 32)
            dve.wait_ge(cexp_ready, 1)
            link(dve.tensor_scalar(CE[:, :, :], CE[:, :, :], 1.0, None, ALU.add))
            link(dve.reciprocal(CE[:, :, :], CE[:, :, :]))
            dve.tensor_tensor(CT[:, :, 0:2].rearrange("p k s -> p s k"), CE[:, :, :], CR[:, :, :], ALU.mult).then_inc(cT_ready, 1)

            def lam(L):
                dve.wait_ge(layer_small_in, 16 * LAYER_DMAS * (L + 1))
                for j in range(2):
                    link(dve.tensor_tensor(JUNK2, LM[:, 2 * j, :], LM[:, 2 * j + 1, :], ALU.mult))
                    ins = dve.tensor_reduce(LAM[:, j:j + 1], JUNK2, AXX, ALU.add)
                    if j == 0:
                        link(ins)
                ins.then_inc(lam_sum, 1)
                dve.wait_ge(lam_exp, L + 1)
                link(dve.tensor_tensor(LAM[:, 4:5], LAM[:, 2:3], LAM[:, 3:4], ALU.subtract))
                link(dve.tensor_scalar(LAM[:, 5:6], LAM[:, 4:5], LAM_INIT[L], None, ALU.add))
                link(dve.tensor_scalar(GAIN[:, :], GAIN[:, :], 1.0 - LAM_INIT[L], None, ALU.mult))

            JUNK2 = JUNK[:, 0:DH]

            def ada_copy(L, cs):
                for c_ in cs:
                    key = ("ada", L, c_)
                    ps = full(dve, key)
                    if c_ >= 2 or L:
                        pc, pL = (c_ - 2, L) if c_ >= 2 else (c_ + 10, L - 1)
                        full(dve, ("mod", pL, pc, mod_streams(pL, pc)[-1]))
                    dve.tensor_copy(R4[:, c_ % 2, :], ps).then_inc(freed(key), 1)

            def modulate(t, done):
                dve.scalar_tensor_tensor(out=HR[:, t, :], in0=SCL[:, t // 2, :], scalar=1.0, in1=X[:, t, :],
                                         op0=ALU.add, op1=ALU.mult).then_inc(done, 1)

            def ask(r, n, src, scale, eps):
                dve.tensor_scalar(VAR[:, r, 0:n], src, scale, eps, ALU.mult, ALU.add).then_inc(S["var_ready"], 1)

            def stats(L, kind, t):
                for hf in range(2):
                    ins = dve.bn_stats(ST[:, hf, :], X[:, t, 512 * hf:512 * hf + 512])
                link(ins)
                link(dve.bn_aggr(MV[:, t, :], ST[:, :, :].rearrange("p a b -> p (a b)")))
                ask(req(L, kind, t), 1, MV[:, t, 1:2], 1.0, LN_EPS)

            def normalise(L, kind, t, done):
                r = req(L, kind, t)
                dve.wait_ge(S["rstd_ready"], r + 1)
                link(dve.tensor_scalar(X[:, t, :], X[:, t, :], MV[:, t, 0:1], RSTD[:, r, 0:1], ALU.subtract, ALU.mult))
                j = 0 if kind == "ln1" else 1
                dve.wait_ge(ln_in, 32 * (2 * L + j + 1))
                dve.tensor_tensor(X[:, t, :], X[:, t, :], LNR[:, 0, :], ALU.mult).then_inc(done, 1)

            def rotate(R, t):
                a, b = CAT["rc"][0] + DH * t, CAT["rs"][0] + DH * t
                cos = C[:, a:a + DH].unsqueeze(1).to_broadcast([P, 8, DH])
                rows = R[:, t, :].rearrange("p (n d) -> p n d", d=DH)
                dve.tensor_tensor(EX[:, 0, :].rearrange("p (n d) -> p n d", d=DH), rows, cos, ALU.mult)
                for o in range(2):
                    sw = R[:, t, :].rearrange("p (n a b i) -> p n a b i", a=2, b=2, i=16)[:, :, :, 1 - o, :]
                    sn = C[:, b:b + DH].rearrange("p (a b i) -> p a b i", a=2, b=2)[:, :, o, :]
                    sn = sn.unsqueeze(1).to_broadcast([P, 8, 2, 16])
                    dst = EX[:, 1, :].rearrange("p (n a b i) -> p n a b i", a=2, b=2, i=16)[:, :, :, o, :]
                    ins = dve.tensor_tensor(dst, sw, sn, ALU.mult)
                link(ins)
                return dve.tensor_tensor(R[:, t, :], EX[:, 0, :], EX[:, 1, :], ALU.add)

            ada_copy(0, [0, 1, 2, 3])
            for L in range(DEPTH):
                T = tiles(L)
                if L == 0:
                    dve.wait_ge(x_in, 32)
                    for c_ in range(4):
                        for r in (0, 1):
                            read(dve, ("mod", 0, c_, r))
                    for t in range(4):
                        modulate(t, S["h1_scaled"])
                key = ("ab", L)
                dve.tensor_copy(AB[:, :, :, :].rearrange("p a b c -> p (a b c)"), full(dve, key)).then_inc(freed(key), 1)
                key = ("swT", L)
                dve.tensor_copy(SWT[:, :, :].rearrange("p a b -> p (a b)"), full(dve, key)).then_inc(freed(key), 1)
                if L == 0:
                    lam(0)
                dve.wait_ge(const_in, 16)
                for t in range(2):
                    read(dve, ("q", L, t))
                    if t:
                        dve.wait_ge(S["q_rot"], val("q_rot", L, t - 1))
                    rotate(QR, t).then_inc(S["q_rot"], 1)
                for t in range(2):
                    read(dve, ("k", L, t))
                    if t:
                        dve.wait_ge(S["k_rot"], val("k_rot", L, t - 1))
                    else:
                        dve.wait_ge(S["q_rot"], val("q_rot", L, 1))
                    rotate(KR, t).then_inc(S["k_rot"], 1)
                for t in range(4):
                    key = ("kT", L, t)
                    ps = full(dve, key)
                    if L and t == 0:
                        dve.wait_ge(S["ln2_done"], val("ln2_done", L - 1, tiles(L - 1) - 1))
                    dve.tensor_copy(KTv[:, :, P * t:P * t + P], ps.rearrange("p (h t) -> p h t", h=HEADS))\
                        .then_inc(freed(key), 1)
                for t in range(T):
                    read(dve, ("g", L, t))
                    link(dve.bn_stats(ST[:, 0, :], GR[:, t, 256:512]))
                    link(dve.bn_aggr(MV[:, t, :], ST[:, 0, :]))
                    ask(req(L, "sgu", t), 1, MV[:, t, 1:2], 1.0, LN_EPS)
                for t in range(T):
                    r = req(L, "sgu", t)
                    dve.wait_ge(S["rstd_ready"], r + 1)
                    v = GR[:, t, 256:512]
                    link(dve.tensor_scalar(v, v, MV[:, t, 0:1], RSTD[:, r, 0:1], ALU.subtract, ALU.mult))
                    link(dve.tensor_tensor(v, v, SG[:, 0, :], ALU.mult))
                    dve.tensor_tensor(v, v, SG[:, 1, :], ALU.add).then_inc(S["sguv_ready"], 1)
                for t in range(T):
                    key = ("fU", L, t)
                    dve.tensor_copy(U[:, t, :, :, :].rearrange("p a b c -> p (a b c)"), full(dve, key))\
                        .then_inc(freed(key), 1)
                for t in range(T):
                    key = ("sg", L, t)
                    ps = full(dve, key)[:, 0:256].rearrange("p (g d) -> p g d", g=4)
                    m = GR[:, t, 256:512]
                    ins = dve.tensor_tensor(m.rearrange("p (g d) -> p g d", g=4), ps,
                                            SB_[:, :].unsqueeze(2).to_broadcast([P, 4, 64]), ALU.add)
                    ins.then_inc(freed(key), 1)
                    read(dve, key)
                    dve.tensor_tensor(GR[:, t, 0:256], GR[:, t, 0:256], m, ALU.mult).then_inc(S["sgu_ready"], 1)
                UN = units(L)

                def maxima(u):
                    nk = 512 if UN[u][0] < 2 else 256
                    if u >= 2:
                        read(dve, ("s", L, u - 2, 1))
                        dve.wait_ge(S["bias_ready"], val("bias_ready", L, u - 2))
                    for cc in range(2):
                        ps = full(dve, ("s", L, u, cc))
                        ins = dve.tensor_reduce(MX[:, u % 2, cc:cc + 1], ps[:, 0:nk], AXX, ALU.max)
                    link(ins)
                    dve.tensor_scalar(NB[:, u % 2, :], MX[:, u % 2, :], -SCALE, None, ALU.mult)\
                        .then_inc(S["bias_ready"], 1)

                def combine(u):
                    nk = 512 if UN[u][0] < 2 else 256
                    p = u % 2
                    for cc in range(2):
                        read(dve, ("s", L, u, cc))
                    if u >= 2:
                        dve.wait_ge(S["a_ready"], val("a_ready", L, u - 2))
                    link(dve.reciprocal(RI[:, p, :], SM[:, p, :]))
                    e0, e1 = EX[:, 2 * p, 0:nk], EX[:, 2 * p + 1, 0:nk]
                    link(dve.tensor_scalar(e1, e1, RI[:, p, 1:2], LAM[:, 5:6], ALU.mult, ALU.mult))
                    dve.scalar_tensor_tensor(out=e0, in0=e0, scalar=RI[:, p, 0:1], in1=e1,
                                             op0=ALU.mult, op1=ALU.subtract).then_inc(S["a_ready"], 1)

                maxima(0)
                maxima(1)
                for u in range(len(UN)):
                    combine(u)
                    if u + 2 < len(UN):
                        maxima(u + 2)
                for t in range(T):
                    for h in range(HEADS):
                        read(dve, ("pv", L, HEADS * t + h))
                    ask(req(L, "att", t), HEADS, SS[:, t, :], 1.0 / P, LN_EPS)
                for t in range(T):
                    r = req(L, "att", t)
                    dve.wait_ge(S["rstd_ready"], r + 1)
                    for h in range(HEADS):
                        o = OB[:, t, P * h:P * h + P]
                        ins = dve.scalar_tensor_tensor(out=o, in0=o, scalar=RSTD[:, r, h:h + 1], in1=GAIN[:, :],
                                                       op0=ALU.mult, op1=ALU.mult)
                    ins.then_inc(S["on_ready"], 1)
                ada_copy(L, [4, 5, 6, 7, 8, 9])
                for c_ in range(4, 10):
                    for r in mod_streams(L, c_):
                        read(dve, ("mod", L, c_, r))
                for step, t in norm_steps(T, "ln1"):
                    if step == "A":
                        for hf in range(2):
                            cs = slice(512 * hf, 512 * hf + 512)
                            key = ("o", L, hf, t)
                            ps = full(dve, key)
                            dve.tensor_tensor(HR[:, t, cs], ps, GT[:, t // 2, cs], ALU.mult).then_inc(freed(key), 1)
                            read(dve, key)
                            ins = dve.scalar_tensor_tensor(out=X[:, t, cs], in0=X[:, t, cs], scalar=ALPHA,
                                                           in1=HR[:, t, cs], op0=ALU.mult, op1=ALU.add)
                        link(ins)
                        stats(L, "ln1", t)
                    elif step == "B":
                        normalise(L, "ln1", t, S["ln1_scaled"])
                    else:
                        dve.wait_ge(S["ln1_done"], val("ln1_done", L, t))
                        modulate(t, S["hx_scaled"])
                for t in range(T):
                    read(dve, ("rt", L, t))
                if L == 0:
                    dve.wait_ge(router_in, 32)
                sc, sl, wk, oh, ga = (b[:, 0:T, :] for b in (SCO, SEL, WK, OH, GATE))
                t1 = T1[:, 0:T, :]
                bc16 = lambda a: a.to_broadcast([P, T, NEXP])
                down16 = cst("down16").unsqueeze(1).to_broadcast([P, T, NEXP])
                down4 = cst("down4").unsqueeze(1).to_broadcast([P, T, 4])
                link(dve.tensor_scalar(sc, ER[:, 0:T, :], 1.0, None, ALU.add))
                link(dve.reciprocal(sc, sc))
                link(dve.tensor_tensor(sl, sc, RBIAS[:, :].unsqueeze(1).to_broadcast([P, T, NEXP]), ALU.add))
                s4 = sl.rearrange("p t (g e) -> p t g e", g=4)
                for n, (a, b) in enumerate([(0, 1), (0, 2), (0, 3), (1, 2), (1, 3), (2, 3)]):
                    ins = dve.tensor_tensor(PG[:, 0:T, n, :], s4[:, :, :, a], s4[:, :, :, b], ALU.add)
                link(ins)
                for n in range(1, 6):
                    link(dve.tensor_tensor(PG[:, 0:T, 0, :], PG[:, 0:T, 0, :], PG[:, 0:T, n, :], ALU.max))
                gs, gm = GS[:, 0:T, :], GM[:, 0:T, :]

                def first_best(src, n, down, w, one_hot):
                    link(dve.tensor_reduce(t1, src, AXX, ALU.max))
                    link(dve.tensor_tensor(w, src, t1.to_broadcast([P, T, n]), ALU.is_equal))
                    link(dve.tensor_tensor(w, w, down, ALU.mult))
                    link(dve.tensor_reduce(t1, w, AXX, ALU.max))
                    link(dve.tensor_tensor(one_hot, w, t1.to_broadcast([P, T, n]), ALU.is_equal))

                first_best(PG[:, 0:T, 0, :], 4, down4, gs, gm)
                link(dve.tensor_tensor(s4, s4, gm.unsqueeze(3).to_broadcast([P, T, 4, 4]), ALU.mult))
                link(dve.tensor_scalar(gm, gm, BIG, -BIG, ALU.mult, ALU.add))
                link(dve.tensor_tensor(s4, s4, gm.unsqueeze(3).to_broadcast([P, T, 4, 4]), ALU.add))
                first_best(sl, NEXP, down16, wk, oh)
                link(dve.scalar_tensor_tensor(out=sl, in0=oh, scalar=-2 * BIG, in1=sl, op0=ALU.mult, op1=ALU.add))
                oh2, mask = OH2[:, 0:T, :], ga
                first_best(sl, NEXP, down16, wk, oh2)
                dve.tensor_tensor(mask, oh2, oh, ALU.add).then_inc(S["mask_ready"], 1)
                wp = WK2[:, 0:T, :]
                for k, o in enumerate((oh, oh2)):
                    link(dve.tensor_tensor(wk, o, sc, ALU.mult))
                    link(dve.tensor_reduce(wp[:, :, k:k + 1], wk, AXX, ALU.add))
                link(dve.tensor_reduce(t1, wp, AXX, ALU.add))
                link(dve.reciprocal(t1, t1))
                link(dve.tensor_tensor(wp, wp, t1.to_broadcast([P, T, 2]), ALU.mult))
                dve.wait_ge(S["mask_ready"], val("mask_ready", L, 0))
                for t in range(T):
                    key = ("rk", L, t)
                    dve.tensor_copy(POS[:, t, :], full(dve, key)[:, 0:NEXP]).then_inc(freed(key), 1)
                    read(dve, key)
                ps, pm = POS[:, 0:T, :], POSM[:, 0:T, :]
                link(dve.tensor_scalar(pm, ps, 1.0, None, ALU.add))
                link(dve.tensor_tensor(pm, pm, mask, ALU.mult))
                link(dve.tensor_scalar(pm, pm, -1.0, None, ALU.add))
                if L == 0:
                    link(dve.memset(IDX[:, :], 0))
                if L == 0:
                    dve.tensor_copy(IOTA16[:, :], C[:, CAT["iota"][0]:CAT["iota"][0] + P])
                    dve.tensor_copy(TOKEN16[:, :, :].rearrange("p t n -> p (t n)"), cst("token2"))
                link(dve.tensor_copy(POS16[:, 0:T, :], pm))
                iota = IOTA16[:, :].unsqueeze(1).to_broadcast([P, 4, P])
                full(dve, ("rt", L, T - 1))
                for g in range(NEXP // 4):
                    for t in range(T):
                        ins = dve.tensor_tensor(PB[:, g, t, :].rearrange("p (e s) -> p e s", e=4), iota,
                                                POS16[:, t, 4 * g:4 * g + 4].unsqueeze(2).to_broadcast([P, 4, P]),
                                                ALU.is_equal)
                    ins.then_inc(S["pick_ready"], 1)
                key = ("ix", L)
                ps_ix = full(dve, key)
                link(dve.tensor_reduce(WK[:, 0, :], ps_ix[:, 0:2 * NEXP].rearrange("p (e n) -> p e n", n=2), AXX, ALU.add))
                dve.tensor_copy(IDX[:, 0:NEXP], WK[:, 0, :]).then_inc(freed(key), 1)
                read(dve, key)
                key = ("ct", L)
                link(dve.memset(CNT[:, :, :], 0.0))
                dve.tensor_copy(CNT[:, 0, 1:17], full(dve, key)[:, 0:NEXP]).then_inc(freed(key), 1)
                read(dve, key)
                for j in range(1, T):
                    link(dve.scalar_tensor_tensor(out=CNT[:, 1, 1:17], in0=CNT[:, 0, 1:17], scalar=float(P * j),
                                                  in1=CNT[:, 1, 1:17], op0=ALU.is_gt, op1=ALU.add))
                link(dve.tensor_scalar(CNT[:, 2, :], CNT[:, 2, :], 1.0, None, ALU.add))
                link(dve.tensor_tensor_scan(CNT[:, 3, :], CNT[:, 2, :], CNT[:, 1, :], 0.0, ALU.mult, ALU.add))
                link(dve.tensor_tensor_scan(CNT[:, 4, :], CNT[:, 2, :], CNT[:, 0, :], 0.0, ALU.mult, ALU.add))
                dve.tensor_copy(META[0:1, L, 0, 0:16], CNT[0:1, 0, 1:17])
                dve.tensor_copy(META[0:1, L, 1, :], CNT[0:1, 3, :])
                dve.tensor_copy(META[0:1, L, 2, :], CNT[0:1, 4, :]).then_inc(spill_step[L], 1)
                link(dve.tensor_tensor(ps, ps, CNT[:, 4, 0:NEXP].unsqueeze(1).to_broadcast([P, T, NEXP]), ALU.add))
                for k, o in enumerate((oh, oh2)):
                    link(dve.tensor_tensor(wk, o, ps, ALU.mult))
                    link(dve.tensor_reduce(DF[:, 0:T, k:k + 1], wk, AXX, ALU.add))
                dve.tensor_copy(DEST[:, 0:T, :], DF[:, 0:T, :]).then_inc(S["dest_ready"], 1)
                mb = MOE_BASE[L]

                def spill_picks(i, p, before, j):
                    v = (before + (j - 1)) * SPILL + 1
                    step = spill_step[L]
                    dve.wait_ge(step, v)
                    a = CAT["iota"][0]
                    for t in range(T):
                        o = a + P if isinstance(j, int) else j * P + a
                        ins = dve.tensor_scalar(PBO[:, t, :], C[:, o:o + P] if isinstance(j, int) else C[:, bass.ds(o, P)],
                                                POSM[:, t, bass.ds(2 * i + p, 1)], None, ALU.is_equal)
                    ins.then_inc(step, 1)
                    dve.wait_ge(step, v + 2)
                    dve.tensor_copy(IXO[:, 0:1], PS[:, 4 * (1 - p), 0:1]).then_inc(step, 1)

                def spill_counts(i, p):
                    return (dve.value_load(META[0:1, L, 0, bass.ds(2 * i + p, 1)], min_val=0, max_val=CAP),
                            dve.value_load(META[0:1, L, 1, bass.ds(2 * i + p, 1)], min_val=0, max_val=7))

                def spill_ahead(i, p):
                    cnt, before = spill_counts(i, p)
                    with dve.If(cnt > P):
                        spill_picks(i, p, before, 1)

                def spill(i, p):
                    cnt, before = spill_counts(i, p)
                    step = spill_step[L]
                    with dve.If(cnt > P):
                        with dve.Fori(1, T) as j:
                            with dve.If(cnt > j * P):
                                v = (before + (j - 1)) * SPILL + 1
                                dve.wait_ge(step, v + 7)
                                dve.tensor_tensor(EX[:, 2 + p, :], PS[:, 2 * p + 1, :], EX[:, p, :], ALU.mult)\
                                    .then_inc(step, 1)
                                dve.wait_ge(step, v + 11)
                                dve.wait_ge(y_written[p], i * 16 + 16 * (PAIRS * L + 2))
                                for hf in range(2):
                                    ins = dve.tensor_copy(YO[:, p, 512 * hf:512 * hf + 512], PS[:, 6 + hf, :])
                                ins.then_inc(step, 1)
                                wait_apart(dve, step, v + SPILL)
                                with dve.If(cnt > (j + 1) * P):
                                    spill_picks(i, p, before, j + 1)
                            with dve.Else():
                                dve.nop()
                        dve.nop()

                dve.wait_ge(spill_step[L], 1)
                with dve.Fori(0, PAIRS) as i:
                    def product(p):
                        b = 2 * p + 1
                        dve.wait_ge(bank_full[b], i + (mb[b] + 1))
                        dve.wait_ge(bank_free[b - 1], i * 2 + (mb[b - 1] + 1))
                        dve.wait_ge(bank_full[b - 1], i * 2 + mb[b - 1])
                        dve.tensor_tensor(EX[:, 2 + p, :], PS[:, b, :], EX[:, p, :], ALU.mult)\
                            .then_inc(bank_free[b], 1)

                    def result(p):
                        dve.wait_ge(bank_full[7], i * 2 + (mb[7] + 1 + p))
                        dve.wait_ge(y_written[p], i * 16 + 16 * (PAIRS * L + 1))
                        dve.tensor_copy(YO[:, p, 512:1024], PS[:, 7, :]).then_inc(bank_free[7], 1)

                    product(0)
                    spill_ahead(i, 0)
                    product(1)
                    result(0)
                    spill(i, 0)
                    spill_ahead(i, 1)
                    result(1)
                    spill(i, 1)
                if L + 1 < DEPTH:
                    lam(L + 1)
                for l, c_ in [(L, 10), (L, 11)] + [(L + 1, c) for c in range(4) if L + 1 < DEPTH]:
                    for r in mod_streams(l, c_):
                        read(dve, ("mod", l, c_, r))
                for step, t in norm_steps(T, "ln2"):
                    if step == "A":
                        dve.wait_ge(g_in[t % 2], 32 * (sum(tiles(l) for l in range(L)) // 2 + t // 2 + 1))
                        g0, g1 = G2[:, t % 2, 0, :], G2[:, t % 2, 1, :]
                        link(dve.tensor_scalar(g0, g0, WK2[:, t, 0:1], None, ALU.mult))
                        link(dve.scalar_tensor_tensor(out=g0, in0=g1, scalar=WK2[:, t, 1:2], in1=g0,
                                                      op0=ALU.mult, op1=ALU.add))
                        link(dve.tensor_tensor(g0, g0, GT[:, t // 2, :], ALU.mult))
                        dve.scalar_tensor_tensor(out=X[:, t, :], in0=X[:, t, :], scalar=ALPHA, in1=g0,
                                                 op0=ALU.mult, op1=ALU.add).then_inc(S["mixed_ready"], 1)
                        dve.wait_ge(S["mixed_ready"], val("mixed_ready", L, t))
                        stats(L, "ln2", t)
                    elif step == "B":
                        normalise(L, "ln2", t, S["ln2_scaled"])
                    elif L + 1 < DEPTH:
                        dve.wait_ge(S["ln2_done"], val("ln2_done", L, t))
                        for n in (t // 2, t // 2 + 2):
                            if n < T and n <= t + 2:
                                dve.wait_ge(S["mixed_ready"], val("mixed_ready", L, n))
                        modulate(t, S["h1_scaled"])

        @block.tensor
        def _(pe):
            def claim(key):
                b, n = BANK[key]
                if n > 1:
                    pe.wait_ge(bank_free[b], n - 1)
                return PS[:, b, :], bank_full[b]

            def weights(key):
                s, n = PLACE[key]
                pe.wait_ge(w_full[s], 16 * n)
                return slot(key)

            def spread(L, c_):
                read(pe, ("ada", L, c_))
                for r in mod_streams(L, c_):
                    ps, done = claim(("mod", L, c_, r))
                    a = CAT["sel"][0] + r
                    pe.matmul(ps, C[:, a:a + 1].to_broadcast([P, P]), R4[:, c_ % 2, :], start=True, stop=True)\
                        .then_inc(done, 1)

            def ada(L, cs):
                for n, c_ in enumerate(cs):
                    ps, done = claim(("ada", L, c_))
                    w = weights(("ada", L, c_))
                    pe.matmul(ps[0:32, :], IDENT[0:12 * DEPTH, 12 * L + c_:12 * L + c_ + 1].to_broadcast([12 * DEPTH, 32]), BA[:, :],
                              start=True, stop=False)
                    for k in range(KD):
                        a = 32 * (k % 4)
                        mm = pe.matmul(ps[a:a + 32, :], CT[:, k, :], w[:, k, :], start=(0 < k < 4), stop=(k >= 4),
                                       tile_position=(0, a))
                    mm.then_inc(done, 1)
                    if n:
                        spread(L, cs[n - 1])
                spread(L, cs[-1])

            def turn(key, pieces):
                ps, done = claim(key)
                for n, piece in enumerate(pieces):
                    mm = pe.transpose(ps[:, P * n:P * n + P], piece, IDENT)
                mm.then_inc(done, 1)

            for L in range(DEPTH):
                T = tiles(L)
                if L == 0:
                    pe.wait_ge(const_in, 16)
                    pe.wait_ge(cT_ready, 1)
                    pe.wait_ge(ba_in, 16)
                    ada(0, [0, 1, 2, 3])
                pe.wait_ge(layer_in, 16 * WF_DMAS * (L + 1))
                ps, done = claim(("ab", L))
                if L:
                    full(pe, ("fU", L - 1, tiles(L - 1) - 1))
                for pr in range(2):
                    for n, m in enumerate(("cc", "sc")):
                        o = P * (2 * pr + n)
                        mm = pe.matmul(ps[:, o:o + P], cst(m), WF[:, pr, :], start=True, stop=True)
                mm.then_inc(done, 1)
                pe.wait_ge(sgu_w_in, 16 * (L + 1))
                turn(("swT", L), [SWR[:, g, :] for g in range(4)])

                def project(name, c0, cw, n, only=None):
                    w = weights(("in", L, name))
                    for t in range(n(L)) if only is None else (only,):
                        for hf in range(2):
                            read(pe, ("hT", L, t, hf))
                        ps, done = claim((name, L, t))
                        for k in range(KD):
                            mm = pe.matmul(ps[:, 0:cw], XT[:, k, P * t:P * t + P], w[:, k, :],
                                           start=(k == 0), stop=(k == KD - 1))
                        mm.then_inc(done, 1)

                for job in first_jobs(L):
                    if job[0] == "hT":
                        t = job[2]
                        pe.wait_ge(S["h1_ready"], val("h1_ready", L, t))
                        for hf in range(2):
                            turn(("hT", L, t, hf), [HR[:, t, 512 * hf + P * k:512 * hf + P * k + P] for k in range(4)])
                    elif job[0] != "skip":
                        project(*CHUNKS["qk".index(job[0])], only=job[2])
                for ch in CHUNKS[2:4]:
                    project(*ch)
                for t in range(T):
                    read(pe, ("q", L, t))
                    if t < 2:
                        pe.wait_ge(S["q_rot"], val("q_rot", L, t))
                    turn(("qT", L, t), [QR[:, t, P * h:P * h + P] for h in range(HEADS)])
                for t in range(4):
                    read(pe, ("k", L, t))
                    if t < 2:
                        pe.wait_ge(S["k_rot"], val("k_rot", L, t))
                    turn(("kT", L, t), [KR[:, t, P * h:P * h + P] for h in range(HEADS)])
                for t in range(T):
                    read(pe, ("f", L, t))
                    turn(("fT", L, t), [FR[:, t, P * a:P * a + P] for a in range(2)])
                project(*CHUNKS[4])
                read(pe, ("ab", L))
                for t in range(T):
                    read(pe, ("fT", L, t))
                    ps, done = claim(("fU", L, t))
                    for pr in range(2):
                        mm = pe.matmul(ps[:, 256 * pr:256 * pr + 256], FT[:, t, pr, :],
                                       AB[:, pr, :, :].rearrange("p b c -> p (b c)"), start=True, stop=True)
                    mm.then_inc(done, 1)
                for s in range(T // 2):
                    for t in (2 * s, 2 * s + 1):
                        read(pe, ("fU", L, t))
                    for pr in range(2):
                        ps, done = claim(("fY", L, s, pr))
                        for n in range(4):
                            kt, m = n // 2, n % 2
                            a = CAT[("cn", "sn")[m]][0] + SEQ * kt
                            mm = pe.matmul(ps[:, 0:SEQ], U[:, 2 * s + kt, pr, m, :], C[:, a:a + SEQ],
                                           start=(n == 0), stop=(n == 3))
                        mm.then_inc(done, 1)
                read(pe, ("swT", L))
                for t in range(T):
                    pe.wait_ge(S["sguv_ready"], val("sguv_ready", L, t))
                    ps, done = claim(("sg", L, t))
                    for g in range(4):
                        mm = pe.matmul(ps[:, 64 * g:64 * g + 64], SWT[:, g, :], GR[:, t, 256 + 64 * g:320 + 64 * g],
                                       start=True, stop=True)
                    mm.then_inc(done, 1)
                UN = units(L)
                for t in range(4):
                    read(pe, ("kT", L, t))

                def scores(u):
                    t, h = UN[u]
                    read(pe, ("qT", L, t))
                    k0 = 0 if t < 2 else 256
                    for cc in range(2):
                        ps, done = claim(("s", L, u, cc))
                        pe.matmul(ps[:, 0:512 - k0], QT[:, cc, h, P * t:P * t + P], KTv[:, h, k0:512],
                                  start=True, stop=True).then_inc(done, 1)

                def results(u):
                    t, h = UN[u]
                    k0 = 0 if t < 2 else 2
                    read(pe, ("aT", L, u))
                    if u == 0:
                        for n in range(4):
                            read(pe, ("v", L, n))
                    ps, done = claim(("pv", L, u))
                    for n in range(4 - k0):
                        mm = pe.matmul(ps[:, 0:P], AT[:, u % 2, P * n:P * n + P], VR[:, k0 + n, P * h:P * h + P],
                                       start=(n == 0), stop=(n == 3 - k0))
                    mm.then_inc(done, 1)

                scores(0)
                scores(1)
                for u, (t, h) in enumerate(UN):
                    if u + 2 < len(UN):
                        scores(u + 2)
                    k0 = 0 if t < 2 else 2
                    pe.wait_ge(S["a_ready"], val("a_ready", L, u))
                    turn(("aT", L, u), [EX[:, 2 * (u % 2), P * n:P * n + P] for n in range(4 - k0)])
                    if u:
                        results(u - 1)
                results(len(UN) - 1)
                for t in range(T):
                    pe.wait_ge(S["sgu_ready"], val("sgu_ready", L, t))
                    turn(("gT", L, t), [GR[:, t, P * a:P * a + P] for a in range(2)])
                for t in range(T):
                    pe.wait_ge(S["on_ready"], val("on_ready", L, t))
                    turn(("mT", L, t), [OB[:, t, P * h:P * h + P] for h in range(HEADS)])
                ada(L, [4, 5, 6, 7, 8, 9])
                for s in range(T // 2):
                    for pr in range(2):
                        read(pe, ("fY", L, s, pr))

                def project_out(t):
                    read(pe, ("gT", L, t))
                    read(pe, ("mT", L, t))
                    for hf in range(2):
                        w = weights(("out", L, hf))
                        ps, done = claim(("o", L, hf, t))
                        for k in range(KD):
                            mm = pe.matmul(ps, XT[:, k, P * t:P * t + P], w[:, k, :],
                                           start=(k == 0), stop=(k == KD - 1))
                        mm.then_inc(done, 1)
                if L == 0:
                    pe.wait_ge(router_in, 32)

                def route(t):
                    for hf in range(2):
                        read(pe, ("xT", L, t, hf))
                    ps, done = claim(("rt", L, t))
                    for k in range(KD):
                        mm = pe.matmul(ps[:, 0:NEXP], XT[:, k, P * t:P * t + P], WR[:, k, :],
                                       start=(k == 0), stop=(k == KD - 1))
                    mm.then_inc(done, 1)

                project_out(0)
                for t in range(T):
                    if t + 1 < T:
                        project_out(t + 1)
                    else:
                        ada(L, [10, 11])
                    pe.wait_ge(S["hx_ready"], val("hx_ready", L, t))
                    for hf in range(2):
                        turn(("xT", L, t, hf), [HR[:, t, 512 * hf + P * k:512 * hf + P * k + P] for k in range(4)])
                    if t:
                        route(t - 1)
                route(T - 1)
                if L + 1 < DEPTH:
                    ada(L + 1, [0])
                pe.wait_ge(S["mask_ready"], val("mask_ready", L, 0))
                one = cst("one").to_broadcast([P, P])
                for t in range(T):
                    ps, done = claim(("rk", L, t))
                    for n in range(t):
                        pe.matmul(ps[:, 0:NEXP], one, GATE[:, n, :], start=(n == 0), stop=False)
                    pe.matmul(ps[:, 0:NEXP], cst("before"), GATE[:, t, :], start=(t == 0), stop=True).then_inc(done, 1)
                ps, done = claim(("ct", L))
                for t in range(T):
                    mm = pe.matmul(ps[:, 0:NEXP], one, GATE[:, t, :], start=(t == 0), stop=(t == T - 1))
                mm.then_inc(done, 1)
                if L + 1 < DEPTH:
                    ada(L + 1, [1])
                ps, done = claim(("ix", L))
                tk = CAT["token"][0]
                for g in range(NEXP // 4):
                    pe.wait_ge(S["pick_ready"], val("pick_ready", L, g))
                    for e in range(4):
                        for t in range(T):
                            o = 2 * (4 * g + e)
                            mm = pe.matmul(ps[:, o:o + 2], PB[:, g, t, P * e:P * e + P], TOKEN16[:, t, :],
                                           start=(t == 0), stop=(t == T - 1))
                mm.then_inc(done, 1)
                if L + 1 < DEPTH:
                    ada(L + 1, [2, 3])
                mb = MOE_BASE[L]
                rb = RING_BASE[L]
                for b in range(8):
                    pe.wait_ge(bank_free[b], mb[b])

                def turn_rows(src, p):
                    for hf in range(2):
                        for n in range(4):
                            o = 512 * hf + P * n
                            mm = pe.transpose(PS[:, 4 + hf, P * n:P * n + P], src[:, o:o + P], IDENT)
                        yield 4 + hf, mm

                def rows(p, gathered, n4):
                    pe.wait_ge(xg_in[p], gathered)
                    for b in (4, 5):
                        pe.wait_ge(bank_free[b], n4(b) - 1)
                    for b, mm in turn_rows(XG[:, p, :], p):
                        mm.then_inc(bank_full[b], 1)

                def up(p, n):
                    s = 3 * p + n
                    for k in range(KD):
                        mm = pe.matmul(PS[:, 2 * p + n, :], XGT[:, p, k, :], moe_up(s)[:, k, :],
                                       start=(k == 0), stop=(k == KD - 1))
                    return mm

                def turn_act(p):
                    for n in range(FE // P):
                        mm = pe.transpose(PS[:, 2 * p, P * n:P * n + P], EX[:, 2 + p, P * n:P * n + P], IDENT)
                    return mm

                def down(p, hf):
                    for k in range(FE // P):
                        mm = pe.matmul(PS[:, 6 + hf, :], AT[:, p, P * k:P * k + P],
                                       moe_down(3 * p + 2)[:, k, 512 * hf:512 * hf + 512],
                                       start=(k == 0), stop=(k == FE // P - 1))
                    return mm

                def spill_numbers(p, before, j):
                    v = (before + (j - 1)) * SPILL + 1
                    pe.wait_ge(spill_step[L], v + 1)
                    for t in range(T):
                        mm = pe.matmul(PS[:, 4 * (1 - p), 0:1], PBO[:, t, :], C[:, tk + t:tk + t + 1],
                                       start=(t == 0), stop=(t == T - 1))
                    mm.then_inc(spill_step[L], 1)

                def spill_counts(i, p):
                    return (pe.value_load(META[0:1, L, 0, bass.ds(2 * i + p, 1)], min_val=0, max_val=CAP),
                            pe.value_load(META[0:1, L, 1, bass.ds(2 * i + p, 1)], min_val=0, max_val=7))

                def spill_ahead(i, p):
                    cnt, before = spill_counts(i, p)
                    with pe.If(cnt > P):
                        spill_numbers(p, before, 1)

                def spill(i, p):
                    cnt, before = spill_counts(i, p)
                    step = spill_step[L]
                    with pe.If(cnt > P):
                        for b in (4, 5):
                            pe.wait_ge(bank_free[b], i * 2 + (mb[b] + 2 + p))
                        for b in (6, 7):
                            pe.wait_ge(bank_free[b], i * 2 + (mb[b] + 1 + p))
                        pe.wait_ge(bank_free[2 * p], i * 2 + (mb[2 * p] + 2))
                        wait_apart(pe, bank_free[2 * p + 1], i + (mb[2 * p + 1] + 1))
                        with pe.Fori(1, T) as j:
                            with pe.If(cnt > j * P):
                                v = (before + (j - 1)) * SPILL + 1
                                pe.wait_ge(step, v + 3)
                                pe.wait_ge(spill_rows_in[L], (before + j) * 16)
                                for b, mm in turn_rows(XGO, p):
                                    pass
                                mm.then_inc(step, 1)
                                pe.wait_ge(step, v + 5)
                                up(p, 0)
                                up(p, 1).then_inc(step, 1)
                                pe.wait_ge(step, v + 8)
                                turn_act(p).then_inc(step, 1)
                                pe.wait_ge(step, v + 10)
                                down(p, 0)
                                down(p, 1).then_inc(step, 1)
                                wait_apart(pe, step, v + 12)
                                with pe.If(cnt > (j + 1) * P):
                                    spill_numbers(p, before, j + 1)
                            with pe.Else():
                                pe.nop()
                        pe.nop()

                pe.wait_ge(spill_step[L], 1)
                rows(0, 16 * (10 * L + 1), lambda b: mb[b] + 1)
                with pe.Fori(0, PAIRS) as i:
                    def first(p):
                        for b in (4, 5):
                            pe.wait_ge(bank_free[b], i * 2 + (mb[b] + 1 + p))
                        for n in range(2):
                            s, b = 3 * p + n, 2 * p + n
                            pe.wait_ge(w_full[s], i * 16 + 16 * (rb[s] + 1))
                            pe.wait_ge(bank_free[b], i * PER[b] + mb[b])
                            up(p, n).then_inc(bank_full[b], 1)

                    def second(p):
                        pe.wait_ge(bank_free[2 * p + 1], i + (mb[2 * p + 1] + 1))
                        turn_act(p).then_inc(bank_full[2 * p], 1)
                        pe.wait_ge(w_full[3 * p + 2], i * 16 + 16 * (rb[3 * p + 2] + 1))
                        pe.wait_ge(bank_free[2 * p], i * 2 + (mb[2 * p] + 2))
                        for hf in range(2):
                            pe.wait_ge(bank_free[6 + hf], i * 2 + (mb[6 + hf] + p))
                            down(p, hf).then_inc(bank_full[6 + hf], 1)

                    first(0)
                    rows(1, i * 16 + 16 * (9 * L + 1), lambda b: i * 2 + (mb[b] + 2))
                    first(1)
                    spill_ahead(i, 0)
                    second(0)
                    spill(i, 0)
                    rows(0, i * 16 + 16 * (10 * L + 2), lambda b: i * 2 + (mb[b] + 3))
                    spill_ahead(i, 1)
                    second(1)
                    spill(i, 1)


_INS = ["x", "c", "ctx", "c_ctx", "w_ada", "b_ada", "w_in", "w_fourier", "diff_lambda", "diff_subln", "sgu_ln_g",
        "sgu_ln_b", "sgu_w", "sgu_b", "w_out", "ln_g", "ln_b", "w_router", "router_bias", "moe_w1", "moe_w3", "moe_w2"]


def kernel(**inputs):
    import numpy as _np
    import concourse.bacc as _bacc
    from concourse import mybir as _mybir
    from concourse.bass_utils import run_bass_kernel_spmd as _run

    nc = _bacc.Bacc("TRN2", target_bir_lowering=False, num_devices=1, dynamic_dma_scratch_size=4096)
    arrays, args = {}, []
    for name in _INS:
        a = _np.ascontiguousarray(inputs[name])
        arrays[f"in_{name}"] = a
        args.append(nc.dram_tensor(f"in_{name}", a.shape, _mybir.dt.from_np(a.dtype), kind="ExternalInput").ap())
    table = constants()[0]
    arrays["in_const"] = table
    args.append(nc.dram_tensor("in_const", table.shape, _mybir.dt.float32, kind="ExternalInput").ap())
    args.append(nc.dram_tensor("out_0", (1, SEQ, D), _mybir.dt.float32, kind="ExternalOutput").ap())
    backbone(nc, *args)
    r = _run(nc, [arrays], core_ids=[0])
    return r.results[0]["out_0"]
```
